# Optimizing a Trainium2 kernel written in Bass

```python
import math
import jax, jax.numpy as jnp
from jax import lax
import numpy as np

D_MODEL = 1024
BATCH = 1
SEQ = 512
DEPTH = 1

ATTN_HEADS = 8
ATTN_HEAD_DIM = 64
ATTN_WIDTH = ATTN_HEADS * ATTN_HEAD_DIM
GMLP_GROUPS = 8
GMLP_GROUP_DIM = 64
GMLP_WIDTH = GMLP_GROUPS * GMLP_GROUP_DIM
MIX_WIDTH = ATTN_WIDTH + GMLP_WIDTH
IN_COLS = 3 * ATTN_WIDTH + 2 * GMLP_WIDTH
Q_BLOCK = 128
GMLP_CHUNK = 128
PEER_HEADS = 8
PEER_N_KEYS = 128
PEER_N_EXPERTS = PEER_N_KEYS * PEER_N_KEYS
PEER_QUERY_DIM = 256
PEER_HALF = PEER_QUERY_DIM // 2
PEER_TOPK = 16
PEER_TOKEN_BLOCK = 128
PLE_DIM = 256
LN_EPS = 1e-5
DEEPNORM_ALPHA = (2.0 * DEPTH) ** 0.25
DEEPNORM_BETA = (8.0 * DEPTH) ** -0.25

kernel_name = "hybrid_sb_attn_gmlp_peer_deepnorm"

def layer_norm(x, g, b):
    xf = x.astype(jnp.float32)
    mu = jnp.mean(xf, axis=-1, keepdims=True)
    var = jnp.mean(jnp.square(xf - mu), axis=-1, keepdims=True)
    y = (xf - mu) * lax.rsqrt(var + LN_EPS)
    return (y * g.astype(jnp.float32) + b.astype(jnp.float32)).astype(x.dtype)

def rms_norm(x, g):
    xf = x.astype(jnp.float32)
    y = xf * lax.rsqrt(jnp.mean(jnp.square(xf), axis=-1, keepdims=True) + LN_EPS)
    return (y * g.astype(jnp.float32)).astype(x.dtype)

def stick_breaking_attention(q, k, v):
    B, S, H, dh = q.shape
    nb = S // Q_BLOCK
    qh = q.transpose(0, 2, 1, 3)
    kh = k.transpose(0, 2, 1, 3)
    vh = v.transpose(0, 2, 1, 3)
    q_blocks = qh.reshape(B, H, nb, Q_BLOCK, dh).transpose(2, 0, 1, 3, 4)
    starts = jnp.arange(nb, dtype=jnp.int32) * Q_BLOCK
    scale = 1.0 / math.sqrt(dh)
    s_idx = jnp.arange(S, dtype=jnp.int32)

    def block(args):
        qb, start = args
        z = jnp.einsum('bhtd,bhsd->bhts', qb, kh).astype(jnp.float32) * scale
        t_idx = start + jnp.arange(Q_BLOCK, dtype=jnp.int32)
        mask = s_idx[None, :] < t_idx[:, None]
        log_beta = jax.nn.log_sigmoid(z)
        log_1m_beta = jnp.where(mask, jax.nn.log_sigmoid(-z), 0.0)
        suffix = lax.cumsum(log_1m_beta, axis=3, reverse=True) - log_1m_beta
        a = jnp.where(mask, jnp.exp(log_beta + suffix), 0.0)
        return jnp.einsum('bhts,bhsd->bhtd', a.astype(vh.dtype), vh)

    out = lax.map(block, (q_blocks, starts))
    return out.transpose(1, 0, 3, 2, 4).reshape(B, S, H * dh)

def gmlp_spatial_gating(u, v, vn_g, vn_b, w_s, b_s):
    B, S, _ = v.shape
    nc = S // GMLP_CHUNK
    v = layer_norm(v, vn_g, vn_b)
    vc = v.reshape(B, nc, GMLP_CHUNK, GMLP_GROUPS, GMLP_GROUP_DIM)
    causal = jnp.tril(jnp.ones((GMLP_CHUNK, GMLP_CHUNK), dtype=w_s.dtype))
    mixed = jnp.einsum('gts,bcsgd->bctgd', w_s * causal[None], vc)
    mixed = mixed + b_s.T[None, None, :, :, None]
    return u * mixed.reshape(B, S, GMLP_WIDTH)

def peer(x, w_q, sub_keys, u_tab, v_tab):
    B, S, D = x.shape
    q = (x @ w_q).reshape(B, S, PEER_HEADS, 2, PEER_HALF)
    scores = jnp.einsum('bshpk,hpnk->bshpn', q, sub_keys).astype(jnp.float32)
    s1, i1 = lax.top_k(scores[:, :, :, 0, :], PEER_TOPK)
    s2, i2 = lax.top_k(scores[:, :, :, 1, :], PEER_TOPK)
    cand = (s1[..., :, None] + s2[..., None, :]).reshape(B, S, PEER_HEADS, PEER_TOPK * PEER_TOPK)
    top_s, top_c = lax.top_k(cand, PEER_TOPK)
    ia = top_c // PEER_TOPK
    ib = top_c % PEER_TOPK
    ids = (jnp.take_along_axis(i1, ia, axis=-1) * PEER_N_KEYS
           + jnp.take_along_axis(i2, ib, axis=-1))
    gates = jax.nn.softmax(top_s, axis=-1).astype(x.dtype)

    T = B * S
    nblk = T // PEER_TOKEN_BLOCK
    xt = x.reshape(nblk, PEER_TOKEN_BLOCK, D)
    idt = ids.reshape(nblk, PEER_TOKEN_BLOCK, PEER_HEADS, PEER_TOPK)
    gt = gates.reshape(nblk, PEER_TOKEN_BLOCK, PEER_HEADS, PEER_TOPK)

    def block(args):
        xb, idb, gb = args
        ue = jnp.take(u_tab, idb, axis=0)
        h = jnp.einsum('thkd,td->thk', ue, xb)
        act = gb * jax.nn.gelu(h, approximate=False)
        ve = jnp.take(v_tab, idb, axis=0)
        return jnp.einsum('thk,thkd->td', act, ve)

    out = lax.map(block, (xt, idt, gt))
    return out.reshape(B, S, D)

def setup_inputs(seed: int = 0) -> dict:
    key = jax.random.key(seed)
    ks = jax.random.split(key, 24)
    f32 = jnp.float32
    n = lambda k, shape, s: jax.random.normal(k, shape, f32) * s
    L = DEPTH
    return {
        "x": n(ks[0], (BATCH, SEQ, D_MODEL), 1.0),
        "p": n(ks[1], (DEPTH, BATCH, SEQ, PLE_DIM), 1.0),
        "w_in": n(ks[2], (L, D_MODEL, IN_COLS), D_MODEL ** -0.5),
        "attn_out_g": 1.0 + n(ks[3], (L, ATTN_WIDTH), 0.05),
        "gmlp_vn_g": 1.0 + n(ks[4], (L, GMLP_WIDTH), 0.05),
        "gmlp_vn_b": n(ks[5], (L, GMLP_WIDTH), 0.02),
        "gmlp_ws": n(ks[6], (L, GMLP_GROUPS, GMLP_CHUNK, GMLP_CHUNK), GMLP_CHUNK ** -0.5),
        "gmlp_bs": 1.0 + n(ks[7], (L, GMLP_GROUPS, GMLP_CHUNK), 0.1),
        "gmlp_out_g": 1.0 + n(ks[8], (L, GMLP_WIDTH), 0.05),
        "w_out": n(ks[9], (L, MIX_WIDTH, D_MODEL), MIX_WIDTH ** -0.5 * DEEPNORM_BETA),
        "ln1_g": 1.0 + n(ks[10], (L, D_MODEL), 0.05),
        "ln1_b": n(ks[11], (L, D_MODEL), 0.02),
        "peer_wq": n(ks[12], (L, D_MODEL, PEER_HEADS * PEER_QUERY_DIM), D_MODEL ** -0.5),
        "peer_subkeys": n(ks[13], (L, PEER_HEADS, 2, PEER_N_KEYS, PEER_HALF), PEER_HALF ** -0.5),
        "peer_u": n(ks[14], (L, PEER_N_EXPERTS, D_MODEL), D_MODEL ** -0.5),
        "peer_v": n(ks[15], (L, PEER_N_EXPERTS, D_MODEL), DEEPNORM_BETA),
        "ln2_g": 1.0 + n(ks[16], (L, D_MODEL), 0.05),
        "ln2_b": n(ks[17], (L, D_MODEL), 0.02),
        "ple_wproj": n(ks[18], (L, PLE_DIM, D_MODEL), PLE_DIM ** -0.5 * DEEPNORM_BETA),
        "ple_wgate": n(ks[19], (L, D_MODEL, D_MODEL), D_MODEL ** -0.5),
        "ple_bgate": n(ks[20], (L, D_MODEL), 0.02),
        "ln3_g": 1.0 + n(ks[21], (L, D_MODEL), 0.05),
        "ln3_b": n(ks[22], (L, D_MODEL), 0.02),
    }

def reference(x, p, w_in, attn_out_g, gmlp_vn_g, gmlp_vn_b, gmlp_ws, gmlp_bs, gmlp_out_g, w_out,
              ln1_g, ln1_b, peer_wq, peer_subkeys, peer_u, peer_v, ln2_g, ln2_b,
              ple_wproj, ple_wgate, ple_bgate, ln3_g, ln3_b):
    B, S, D = x.shape
    for i in range(DEPTH):
        h = x @ w_in[i]
        q, k, v, gu, gv = jnp.split(
            h, [ATTN_WIDTH, 2 * ATTN_WIDTH, 3 * ATTN_WIDTH, 3 * ATTN_WIDTH + GMLP_WIDTH], axis=-1)
        hs = (B, S, ATTN_HEADS, ATTN_HEAD_DIM)
        attn = stick_breaking_attention(q.reshape(hs), k.reshape(hs), v.reshape(hs))
        attn = rms_norm(attn, attn_out_g[i])
        gm = gmlp_spatial_gating(jax.nn.gelu(gu, approximate=False), jax.nn.gelu(gv, approximate=False),
                                 gmlp_vn_g[i], gmlp_vn_b[i], gmlp_ws[i], gmlp_bs[i])
        gm = rms_norm(gm, gmlp_out_g[i])
        mix = jnp.concatenate([attn, gm], axis=-1) @ w_out[i]
        x = layer_norm(DEEPNORM_ALPHA * x + mix, ln1_g[i], ln1_b[i])
        ffn = peer(x, peer_wq[i], peer_subkeys[i], peer_u[i], peer_v[i])
        x = layer_norm(DEEPNORM_ALPHA * x + ffn, ln2_g[i], ln2_b[i])
        gate = jax.nn.sigmoid(x @ ple_wgate[i] + ple_bgate[i])
        ple = gate * (p[i] @ ple_wproj[i])
        x = layer_norm(DEEPNORM_ALPHA * x + ple, ln3_g[i], ln3_b[i])
    return x


_drawn_inputs = setup_inputs


def setup_inputs(seed=0):
    import zlib

    import numpy as np

    out = dict(_drawn_inputs(seed))
    spreads = {}
    factors = {'gmlp_vn_b': 3.793, 'ln2_b': 2.969, 'ple_bgate': 29.207, 'ln3_b': 2.835}
    for name, (base, spread) in spreads.items():
        noise = np.random.default_rng([zlib.crc32(name.encode()), seed]).standard_normal(out[name].shape)
        drawn = base * np.exp(spread * noise) if base else spread * noise
        out[name] = __import__('jax').numpy.asarray(drawn.astype(out[name].dtype))
    for name, factor in factors.items():
        out[name] = (out[name] * factor).astype(out[name].dtype)
    return out
```

```python
import math
from contextlib import ExitStack

import numpy as np
import concourse.bass as bass
from concourse import mybir

FP32 = mybir.dt.float32
U32 = mybir.dt.uint32
I32 = mybir.dt.int32
ALU = mybir.AluOpType
ACT = mybir.ActivationFunctionType
AX = mybir.AxisListType

P = 128
D = 1024
S = 512
NT = S // P
KD = D // P
AH, DH = 8, 64
AW = AH * DH
G = 8
WB = AW // P
PH, TOPK, NKEY = 8, 16, 128
QD = 256
PLE = 256
EPS = 1e-5
ALPHA = 2.0 ** 0.25
QSCALE = 1.0 / math.sqrt(DH)
NEG = -3.0e38

RING = 8
GRP = 2
NG = TOPK // GRP
RANK_STEPS = 18
HEAD_STEPS = NT * (RANK_STEPS + 1)
DIAGS = 4
HALF = D // 2

ZOFF = {0: 0, 1: 512, 3: 896, 2: 1024}
ZCOLS = 1280


def zlen(s):
    return S - P * s


class Counter:

    def __init__(self, sem):
        self.sem, self.n, self.base = sem, 0, 0

    def inc(self, instruction, by=1):
        instruction.then_inc(self.sem, by)
        self.n += by


def hold(eng, sem, value, passed):
    eng.wait_ge(sem, value)
    eng.sem_inc(passed, 1)


def build(nc, a, out):
    ctx = ExitStack()
    with ctx:
        def sb(name, shape, dt=FP32):
            return ctx.enter_context(nc.sbuf_tensor(name, shape, dt))

        def sem(name):
            return ctx.enter_context(nc.semaphore(name))

        x1 = sb("x1", [P, NT, D])
        x1T = sb("x1T", [P, KD, S])
        wq_head = sb("wq_head", [P, KD, QD])
        subk = sb("subk", [P, PH * 2 * NKEY])
        ident = sb("ident", [P, P])
        neg_tri = sb("neg_tri", [P, P])
        neg_one = sb("neg_one", [P, P])
        ones = sb("ones", [P, 1])
        iota16 = sb("iota16", [P, TOPK])
        gA = sb("gA", [P, WB])
        gG = sb("gG", [P, WB])
        stats = sb("stats", [P, 4, 6])
        aggr = sb("aggr", [P, 4, 2])
        var_e = sb("var_e", [P, 8])
        std = sb("std", [P, 8])
        rinv = sb("rinv", [P, 8])
        rtmp = sb("rtmp", [P, 8])
        rstd = sb("rstd", [P, 8])
        rsn = sb("rsn", [P, 2 * NT])

        arena = sb("arena", [P, 36864])
        at = [0]

        def take(n):
            at[0] += n
            return arena[:, at[0] - n:at[0]]

        ring_w = take(8192)
        wgrp = [ring_w[:, 0:4096], ring_w[:, 4096:8192]]
        w_out = ring_w.rearrange("p (c n) -> p c n", c=8)
        ln1_g, ln1_b = take(D), take(D)
        xT_flat = take(4096)
        xT = xT_flat.rearrange("p (k s) -> p k s", k=KD)
        squares = xT_flat.rearrange("p (c s) -> p c s", c=8)
        qk_flat = take(4096)
        qT = qk_flat[:, 0:2048].rearrange("p (b s) -> p b s", b=WB)
        kT = qk_flat[:, 2048:4096].rearrange("p (b s) -> p b s", b=WB)
        x_nat = qk_flat.rearrange("p (t d) -> p t d", t=NT)
        guT = take(2048).rearrange("p (b s) -> p b s", b=WB)
        v_tok = take(2048).rearrange("p (t c) -> p t c", t=NT)
        gv = take(2048).rearrange("p (t c) -> p t c", t=NT)
        attnT = take(2048).rearrange("p (b s) -> p b s", b=WB)
        gmT = take(2048).rearrange("p (b s) -> p b s", b=WB)
        wsT = take(1024).rearrange("p (g t) -> p g t", g=G)
        vn_g, vn_b = take(AW), take(AW)
        bs_b = take(AW).rearrange("p (b t) -> p b t", b=WB)
        e_buf = take(2 * ZCOLS).rearrange("p (i n) -> p i n", i=2)
        l_buf = take(2 * ZCOLS).rearrange("p (i n) -> p i n", i=2)

        at[0] = 0
        rows = take(RING * 2 * D).rearrange("p (r n) -> p r n", r=RING)
        acc = take(NT * D).rearrange("p (t d) -> p t d", t=NT)
        w_gate = take(KD * D).rearrange("p (k n) -> p k n", k=KD)
        w_proj = take(2 * D).rearrange("p (k n) -> p k n", k=2)
        ln2_g, ln2_b, ln3_g, ln3_b, b_gate = (take(D) for _ in range(5))
        pT = take(2 * S).rearrange("p (k s) -> p k s", k=2)
        assert at[0] <= 36864

        qs = sb("qs", [P, QD])
        left = sb("left", [P, 2, NKEY])
        top = sb("top", [P, 2, TOPK])
        topi = sb("topi", [P, 2, TOPK], U32)
        topf = sb("topf", [P, 2, TOPK])
        cand = sb("cand", [P, TOPK * TOPK])
        cleft = sb("cleft", [P, TOPK * TOPK])
        best = sb("best", [P, NT, TOPK])
        besti = sb("besti", [P, TOPK], U32)
        nib = sb("nib", [P, 2, TOPK], U32)
        nibf = sb("nibf", [P, 2, TOPK])
        hot = sb("hot", [P, 2, TOPK, TOPK])
        pick = sb("pick", [P, 2, TOPK])
        ids = sb("ids", [P, NT, TOPK], I32)
        negmax = sb("negmax", [P, NT])
        expv = sb("expv", [P, NT, TOPK])
        esum = sb("esum", [P, NT])
        erec = sb("erec", [P, NT])
        gates = sb("gates", [P, NT, TOPK])
        hid = sb("hid", [P, NT, TOPK])
        gel = sb("gel", [P, NT, TOPK])
        actv = sb("actv", [P, NT, TOPK])
        diag = sb("diag", [P, DIAGS, P])

        ps = ctx.enter_context(nc.psum_tensor("ps", [P, 8, 512], FP32))
        psf = ps[:, :, :].rearrange("p b n -> p (b n)")

        xT_in = sem("xT_in")
        w_in = [sem(f"w_in{i}") for i in range(8)]
        small_in = sem("small_in")
        wout_in = [sem("wout_in0"), sem("wout_in1")]
        x_in = sem("x_in")
        ln1_in = sem("ln1_in")
        subk_in = sem("subk_in")
        wq_in = sem("wq_in")
        tail_in = sem("tail_in")
        const_ready = sem("const_ready")
        ws_masked = sem("ws_masked")
        proj_done = sem("proj_done")
        act_evac = sem("act_evac")
        dve_evac = sem("dve_evac")
        z_done = sem("z_done")
        log_ready = sem("log_ready")
        l_ready = sem("l_ready")
        l_masked = sem("l_masked")
        arg_done = sem("arg_done")
        a_ready = sem("a_ready")
        a_masked = sem("a_masked")
        av_done = sem("av_done")
        attn_sq = sem("attn_sq")
        attn_scaled = sem("attn_scaled")
        gvn_ready = sem("gvn_ready")
        mixed_done = sem("mixed_done")
        gm_ready = sem("gm_ready")
        gm_out = sem("gm_out")
        ssq_done = sem("ssq_done")
        rms_ready = sem("rms_ready")
        wout_done = sem("wout_done")
        pa_scaled = sem("pa_scaled")
        x1_ready = sem("x1_ready")
        x1_tr = sem("x1_tr")
        x1T_ready = sem("x1T_ready")
        var_ready = sem("var_ready")
        std_ready = sem("std_ready")
        dve_at = sem("dve_at")
        act_at = sem("act_at")

        q_done = sem("q_done")
        qs_ready = sem("qs_ready")
        score_done = sem("score_done")
        score_used = sem("score_used")
        ids_ready = sem("ids_ready")
        exp_ready = sem("exp_ready")
        gates_ready = sem("gates_ready")
        rows_in = [sem(f"rows_in{i}") for i in range(RING)]
        dots_done = sem("dots_done")
        gel_ready = sem("gel_ready")
        actv_ready = sem("actv_ready")
        diag_ready = sem("diag_ready")
        slot_free = sem("slot_free")
        sum_free = sem("sum_free")
        x2_ready = sem("x2_ready")
        x2_tr = sem("x2_tr")
        x2T_ready = sem("x2T_ready")
        ple_done = sem("ple_done")
        gate_in = sem("gate_in")
        gate_ready = sem("gate_ready")
        ple_used = sem("ple_used")
        out_ready = sem("out_ready")
        out_done = sem("out_done")
        dve_passed = sem("dve_passed")
        pool_passed = sem("pool_passed")

        block = ctx.enter_context(nc.Block())

        @block.sync
        def _(sp):
            sp.dma_start(xT, a["xT"][:, :, :]).then_inc(xT_in, 16)
            for b in range(WB):
                sp.dma_start(wgrp[0][:, b * D:(b + 1) * D],
                             a["w_q"][:, b * D:(b + 1) * D]).then_inc(w_in[b], 16)
            sp.dma_start(wgrp[1], a["w_k"][:, :]).then_inc(w_in[4], 16)
            sp.dma_start(wsT, a["wsT"][:, :, :]).then_inc(small_in, 16)
            sp.dma_start(vn_g, a["gmlp_vn_g"][0, :].partition_broadcast(P)).then_inc(small_in, 16)
            sp.dma_start(vn_b, a["gmlp_vn_b"][0, :].partition_broadcast(P)).then_inc(small_in, 16)
            for half in range(2):
                sp.dma_start(bs_b[half * DH:(half + 1) * DH, :, :],
                             a["gmlp_bs"][0].rearrange("(b h) t -> h b t", h=2)[half]
                             .partition_broadcast(DH)).then_inc(small_in, 16)
            sp.dma_start(gA[:, :], a["gA"][:, :]).then_inc(small_in, 16)
            sp.dma_start(gG[:, :], a["gG"][:, :]).then_inc(small_in, 16)
            sp.dma_start(subk[:, :], a["subk"][:, :]).then_inc(subk_in, 16)
            sp.dma_start(wq_head[:, :, :], a["wq"][0]).then_inc(wq_in, 16)
            sp.wait_ge(proj_done, 4)
            sp.dma_start(wgrp[0], a["w_gv"][:, :]).then_inc(w_in[5], 16)
            sp.wait_ge(proj_done, 8)
            sp.dma_start(wgrp[1], a["w_gu"][:, :]).then_inc(w_in[6], 16)
            sp.wait_ge(proj_done, 12)
            sp.dma_start(wgrp[0], a["w_v"][:, :]).then_inc(w_in[7], 16)
            sp.dma_start(ln1_g, a["ln1_g"][0, :].partition_broadcast(P)).then_inc(ln1_in, 16)
            sp.dma_start(ln1_b, a["ln1_b"][0, :].partition_broadcast(P)).then_inc(ln1_in, 16)
            sp.wait_ge(proj_done, 16)
            sp.dma_start(w_out[:, 4:8, :], a["w_out"][:, 4:8, :]).then_inc(wout_in[1], 16)
            sp.wait_ge(proj_done, 20)
            sp.dma_start(w_out[:, 0:4, :], a["w_out"][:, 0:4, :]).then_inc(wout_in[0], 16)
            sp.wait_ge(arg_done, AH)
            sp.dma_start(x_nat, a["x"][:, :, :]).then_inc(x_in, 16)
            sp.wait_ge(x1T_ready, NT)
            for dst, src in ((w_gate, a["w_gate"][:, :, :]), (w_proj, a["w_proj"][:, :, :]), (pT, a["pT"][:, :, :])):
                sp.dma_start(dst, src).then_inc(tail_in, 16)
            for dst, name in ((ln2_g, "ln2_g"), (ln2_b, "ln2_b"), (ln3_g, "ln3_g"), (ln3_b, "ln3_b"),
                              (b_gate, "ple_bgate")):
                sp.dma_start(dst, a[name][0, :].partition_broadcast(P)).then_inc(tail_in, 16)
            with sp.Fori(0, PH - 1) as h:
                sp.wait_ge(q_done, h * NT + NT)
                sp.dma_start(wq_head[:, :, :], a["wq"][bass.ds(h + 1, 1)].rearrange("h p k n -> (h p) k n"))\
                  .then_inc(wq_in, 16)
            for t in range(NT):
                sp.wait_ge(out_ready, t + 1)
                sp.dma_start(out[0, t * P:(t + 1) * P, :], acc[:, t, :]).then_inc(out_done, 16)
            sp.wait_ge(out_done, 16 * NT)

        @block.gpsimd
        def _(pool):
            nc.gpsimd.memset(ident[:, :], 0.0).then_inc(const_ready, 1)
            nc.gpsimd.memset(neg_tri[:, :], -1.0).then_inc(const_ready, 1)
            nc.gpsimd.memset(neg_one[:, :], -1.0).then_inc(const_ready, 1)
            nc.gpsimd.memset(ones[:, :], 1.0).then_inc(const_ready, 1)
            nc.gpsimd.iota(iota16[:, :], pattern=[[1, TOPK]], base=0, channel_multiplier=0,
                           allow_small_or_imprecise_dtypes=True).then_inc(const_ready, 1)
            pool.wait_ge(const_ready, 5)
            nc.gpsimd.affine_select(out=ident[:, :], in_=ident[:, :], compare_op=ALU.not_equal, fill=1.0,
                                    base=0, pattern=[[-1, P]], channel_multiplier=1).then_inc(const_ready, 1)
            nc.gpsimd.affine_select(out=neg_tri[:, :], in_=neg_tri[:, :], compare_op=ALU.is_ge, fill=0.0,
                                    base=0, pattern=[[-1, P]], channel_multiplier=1).then_inc(const_ready, 1)
            pool.wait_ge(small_in, 16 * 7)
            nc.gpsimd.affine_select(out=wsT, in_=wsT, compare_op=ALU.is_ge, fill=0.0, base=0,
                                    pattern=[[0, G], [1, P]], channel_multiplier=-1).then_inc(ws_masked, 1)

            def keep_past(buf, s, done, last):
                blk = buf[:, ZOFF[s]:ZOFF[s] + P]
                i = nc.gpsimd.affine_select(out=blk, in_=blk, compare_op=ALU.is_gt, fill=0.0, base=0,
                                            pattern=[[1, P]], channel_multiplier=-1)
                i.then_inc(done, 1)

            for h in range(AH + 1):
                if h < AH:
                    pool.wait_ge(l_ready, h + 1)
                    for s in range(NT):
                        keep_past(l_buf[:, h % 2, :], s, l_masked, s == NT - 1)
                if h >= 1:
                    pool.wait_ge(a_ready, h)
                    for s in range(NT):
                        keep_past(e_buf[:, (h - 1) % 2, :], s, a_masked, s == NT - 1)

            def gather_unit(u, t):
                pool.wait_ge(ids_ready, u + 1)
                for c in range(TOPK):
                    hold(pool, slot_free, u * TOPK + c + 1, pool_passed)
                    nc.gpsimd.indirect_dma_start(
                        out=rows[:, c % RING, :], out_offset=None, in_=a["uv"][:, :],
                        in_offset=bass.IndirectOffsetOnAxis(ap=ids[:, t, c:c + 1], axis=0),
                    ).then_inc(rows_in[c % RING], 16)

            with pool.Fori(0, PH) as h:
                for t in range(NT):
                    gather_unit(h * NT + t, t)

        @block.tensor
        def _(pe):
            mm = nc.tensor.matmul

            def project_T(blk, w, j):
                for k in range(KD):
                    i = mm(ps[:, blk % 8, :], w[:, j * D + k * P:j * D + (k + 1) * P], xT[:, k, :],
                           start=(k == 0), stop=(k == KD - 1))
                i.then_inc(proj_done, 1)

            def project_tok(blk, w, t):
                for k in range(KD):
                    i = mm(ps[:, blk % 8, :], xT[:, k, t * P:(t + 1) * P], w[:, k * AW:(k + 1) * AW],
                           start=(k == 0), stop=(k == KD - 1))
                i.then_inc(proj_done, 1)

            pe.wait_ge(xT_in, 16)
            for b in range(WB):
                pe.wait_ge(w_in[b], 16)
                project_T(b, wgrp[0], b)
            pe.wait_ge(w_in[4], 16)
            for b in range(WB):
                project_T(4 + b, wgrp[1], b)
            pe.wait_ge(w_in[5], 16)
            for t in range(NT):
                pe.wait_ge(act_evac, t + 1)
                project_tok(8 + t, wgrp[0], t)
            pe.wait_ge(w_in[6], 16)
            for b in range(WB):
                pe.wait_ge(dve_evac, b + 1)
                project_T(12 + b, wgrp[1], b)
            pe.wait_ge(w_in[7], 16)
            for t in range(NT):
                pe.wait_ge(act_evac, 4 + t + 1)
                project_tok(16 + t, wgrp[0], t)

            def z_cols(h, s, n0=0):
                base = (h % 2) * 3 * 512 + ZOFF[s]
                return psf[:, base + n0:base + zlen(s)]

            def scores(h, s, start):
                r = slice(DH * (h % 2), DH * (h % 2) + DH)
                return mm(z_cols(h, s), kT[r, h // 2, s * P:(s + 1) * P], qT[r, h // 2, s * P:S],
                          start=start, stop=False, skip_group_check=True)

            def open_scores(h):
                if h >= 2:
                    pe.wait_ge(a_ready, h - 1)
                for s in (0, 1, 3, 2):
                    i = scores(h, s, s != 3)
                i.then_inc(z_done, 1)

            pe.wait_ge(act_evac, 12)
            pe.wait_ge(dve_evac, 8)
            pe.wait_ge(const_ready, 7)
            open_scores(0)
            for h in range(AH):
                if h + 1 < AH:
                    open_scores(h + 1)
                pe.wait_ge(l_masked, NT * (h + 1))
                for s in (0, 1, 3, 2):
                    for j in range(s, NT):
                        n0 = (j - s) * P
                        i = mm(z_cols(h, s, n0), (neg_tri if j == s else neg_one)[:, :],
                               l_buf[:, h % 2, ZOFF[j]:ZOFF[j] + zlen(j)], start=False,
                               stop=(j == NT - 1), skip_group_check=True)
                i.then_inc(arg_done, 1)
                pe.wait_ge(a_masked, NT * (h + 1))
                if h >= 4 and h % 2 == 0:
                    pe.wait_ge(attn_sq, h // 2 - 1)
                    pe.wait_ge(attn_scaled, h // 2 - 1)
                r = slice(DH * (h % 2), DH * (h % 2) + DH)
                for s in range(NT):
                    i = mm(ps[r, 6 + (h // 2) % 2, s * P:S], v_tok[:, s, h * DH:(h + 1) * DH],
                           e_buf[:, h % 2, ZOFF[s]:ZOFF[s] + zlen(s)], start=(s == 0), stop=(s == NT - 1),
                           skip_group_check=True)
                i.then_inc(av_done, 1)

            pe.wait_ge(ws_masked, 1)
            pe.wait_ge(gvn_ready, 1)
            for b in range(WB):
                for g in (2 * b, 2 * b + 1):
                    r = slice(DH * (g % 2), DH * (g % 2) + DH)
                    for t in range(NT):
                        i = mm(ps[r, b, t * P:(t + 1) * P], gv[:, t, g * DH:(g + 1) * DH], wsT[:, g, :],
                               start=(t == 0), stop=True, skip_group_check=True)
                i.then_inc(mixed_done, 1)

            pe.wait_ge(attn_sq, WB)
            for kind in range(2):
                if kind == 1:
                    pe.wait_ge(gm_out, WB)
                for t in range(NT):
                    for c in range(WB):
                        i = mm(ps[:, 4, kind * NT + t:kind * NT + t + 1],
                               squares[:, kind * WB + c, t * P:(t + 1) * P], ones[:, :],
                               start=(c == 0), stop=(c == WB - 1))
            i.then_inc(ssq_done, 1)

            def project_out(t):
                for kind, src in ((0, attnT), (1, gmT)):
                    for j in range(2):
                        for c in range(WB):
                            i = mm(ps[:, (t % 2) * 4 + 2 * kind + j, :], src[:, c, t * P:(t + 1) * P],
                                   w_out[:, kind * WB + c, j * HALF:(j + 1) * HALF],
                                   start=(c == 0), stop=(c == WB - 1))
                i.then_inc(wout_done, 1)

            def transpose_x1(t):
                pe.wait_ge(x1_ready, t + 1)
                for k in range(KD):
                    i = nc.tensor.transpose(ps[:, (t % 2) * 4 + k // 4, (k % 4) * P:(k % 4 + 1) * P],
                                            x1[:, t, k * P:(k + 1) * P], ident[:, :])
                i.then_inc(x1_tr, 1)

            pe.wait_ge(wout_in[0], 16)
            pe.wait_ge(wout_in[1], 16)
            pe.wait_ge(attn_scaled, WB)
            project_out(0)
            pe.wait_ge(rms_ready, 1)
            for t in range(1, NT):
                if t >= 2:
                    pe.wait_ge(x1T_ready, t - 1)
                project_out(t)
                transpose_x1(t - 1)
            transpose_x1(NT - 1)

            def query(h, t, u):
                if t == 0:
                    pe.wait_ge(wq_in, h * 16 + 16)
                pe.wait_ge(qs_ready, u)
                for half in range(2):
                    for k in range(KD):
                        i = mm(ps[:, 4, half * P:(half + 1) * P], wq_head[:, k, half * P:(half + 1) * P],
                               x1T[:, k, t * P:(t + 1) * P], start=(k == 0), stop=(k == KD - 1))
                i.then_inc(q_done, 1)

            def key_scores(h, t, u):
                pe.wait_ge(qs_ready, u + 1)
                pe.wait_ge(score_used, u)
                for half in range(2):
                    i = mm(ps[:, 5, half * P:(half + 1) * P], qs[:, half * P:(half + 1) * P],
                           subk[:, bass.ds((h * 2 + half) * NKEY, NKEY)], start=True, stop=True)
                i.then_inc(score_done, 1)

            def combine(u, t, c):
                if c == 0:
                    pe.wait_ge(sum_free, u + 1)
                pe.wait_ge(diag_ready, u * TOPK + c + 1)
                for j in range(2):
                    i = mm(ps[:, 2 * (t % 2) + j, :], diag[:, c % DIAGS, :],
                           rows[:, c % RING, D + j * HALF:D + (j + 1) * HALF],
                           start=(c == 0), stop=(c == TOPK - 1))
                i.then_inc(slot_free, 1)

            def x2_transposes(t):
                pe.wait_ge(x2_ready, t + 1)
                if t:
                    pe.wait_ge(ple_used, 2 * t)
                for k in range(KD):
                    i = nc.tensor.transpose(ps[:, 6 + k // 4, (k % 4) * P:(k % 4 + 1) * P],
                                            acc[:, t, k * P:(k + 1) * P], ident[:, :])
                i.then_inc(x2_tr, 1)

            def ple_products(t, j):
                if t == 0 and j == 0:
                    pe.wait_ge(tail_in, 16 * 8)
                if j == 0:
                    pe.wait_ge(x2T_ready, t + 1)
                else:
                    pe.wait_ge(ple_used, 2 * t + 1)
                for k in range(KD):
                    mm(ps[:, 6, :], x1T[:, k, t * P:(t + 1) * P], w_gate[:, k, j * HALF:(j + 1) * HALF],
                       start=(k == 0), stop=(k == KD - 1))
                for k in range(2):
                    i = mm(ps[:, 7, :], pT[:, k, t * P:(t + 1) * P], w_proj[:, k, j * HALF:(j + 1) * HALF],
                           start=(k == 0), stop=(k == 1))
                i.then_inc(ple_done, 1)

            pe.wait_ge(subk_in, 16)
            pe.wait_ge(x1T_ready, NT)
            query(0, 0, 0)
            key_scores(0, 0, 0)
            query(0, 1, 1)
            key_scores(0, 1, 1)

            def unit(h, t, last_head):
                u = h * NT + t
                ahead = (h, t + 2, u + 2) if t + 2 < NT else (h + 1, t + 2 - NT, u + 2)
                more = not (last_head and t + 2 >= NT)
                for c in range(TOPK):
                    combine(u, t, c)
                    if c == 9 and more:
                        query(*ahead)
                    if c == 11 and more:
                        key_scores(*ahead)
                    if last_head and t:
                        if c == 7:
                            x2_transposes(t - 1)
                        if c == 11:
                            ple_products(t - 1, 0)
                        if c == 15:
                            ple_products(t - 1, 1)

            nc.tensor.matmul(ps[:, 7, 0:1], ident[:, :], ones[:, :], start=True, stop=True)\
              .then_inc(slot_free, RING)
            with pe.Fori(0, PH - 1) as h:
                for t in range(NT):
                    unit(h, t, False)
            for t in range(NT):
                unit(PH - 1, t, True)
            x2_transposes(NT - 1)
            ple_products(NT - 1, 0)
            ple_products(NT - 1, 1)

        @block.scalar
        def _(act):
            fn = nc.scalar.activation
            for b in range(WB):
                act.wait_ge(proj_done, b + 1)
                fn(qT[:, b, :], ps[:, b, :], ACT.Copy, scale=QSCALE).then_inc(act_evac, 1)
            for t in range(NT):
                act.wait_ge(proj_done, 8 + t + 1)
                fn(gv[:, t, :], ps[:, t, :], ACT.Gelu).then_inc(act_evac, 1)
            for b in range(WB):
                act.wait_ge(proj_done, 12 + b + 1)
                fn(guT[:, b, :], ps[:, 4 + b, :], ACT.Gelu).then_inc(act_evac, 1)
            stds = Counter(std_ready)

            def sqrt_var(n):
                act.wait_ge(var_ready, stds.n + 1)
                stds.inc(fn(std[:, 0:n], var_e[:, 0:n], ACT.Sqrt))

            sqrt_var(NT)
            for h in range(AH + 1):
                if h < AH:
                    e = e_buf[:, h % 2, :]
                    act.wait_ge(z_done, h + 1)
                    if h >= 2:
                        act.wait_ge(av_done, h - 1)
                    z = psf[:, (h % 2) * 1536:(h % 2) * 1536 + ZCOLS]
                    fn(e, z, ACT.Abs).then_inc(act_at, 1)
                    act.wait_ge(act_at, 2 * h + 1)
                    fn(e, e, ACT.Exp, scale=-1.0).then_inc(act_at, 1)
                    act.wait_ge(act_at, 2 * h + 2)
                    fn(e, e, ACT.Ln, bias=1.0).then_inc(log_ready, 1)
                if h >= 1:
                    g = h - 1
                    act.wait_ge(arg_done, g + 1)
                    fn(e_buf[:, g % 2, :], psf[:, (g % 2) * 1536:(g % 2) * 1536 + ZCOLS], ACT.Exp)\
                        .then_inc(a_ready, 1)
                    if g % 2 == 0 and g >= 2:
                        b = g // 2 - 1
                        act.wait_ge(av_done, g)
                        fn(squares[:, b, :], ps[:, 6 + b % 2, :], ACT.Square).then_inc(attn_sq, 1)
            act.wait_ge(av_done, AH)
            fn(squares[:, WB - 1, :], ps[:, 6 + (WB - 1) % 2, :], ACT.Square).then_inc(attn_sq, 1)
            for b in range(WB):
                act.wait_ge(gm_ready, b + 1)
                fn(squares[:, WB + b, :], guT[:, b, :], ACT.Square)
                fn(gmT[:, b, :], guT[:, b, :], ACT.Copy, scale=gG[:, b:b + 1]).then_inc(gm_out, 1)
            sqrt_var(2 * NT)

            def scaled_attn(t):
                act.wait_ge(wout_done, t + 1)
                act.wait_ge(rms_ready, 1)
                fn(x1[:, t, :], psf[:, (t % 2) * 2048:(t % 2) * 2048 + D], ACT.Copy,
                   scale=rsn[:, t:t + 1]).then_inc(pa_scaled, 1)

            def keep_x1T(t):
                act.wait_ge(x1_tr, t + 1)
                fn(x1T[:, :, t * P:(t + 1) * P],
                   psf[:, (t % 2) * 2048:(t % 2) * 2048 + D].rearrange("p (k n) -> p k n", k=KD),
                   ACT.Copy).then_inc(x1T_ready, 1)

            scaled_attn(0)
            for t in range(NT):
                sqrt_var(1)
                if t + 1 < NT:
                    if t + 1 < 2:
                        scaled_attn(t + 1)
                keep_x1T(t)
                if 2 <= t + 2 < NT:
                    scaled_attn(t + 2)

            def keep_query(u):
                act.wait_ge(q_done, u + 1)
                act.wait_ge(score_done, u)
                fn(qs[:, :], ps[:, 4, 0:QD], ACT.Copy).then_inc(qs_ready, 1)

            def gate_exp(u, t):
                act.wait_ge(ids_ready, u + 1)
                fn(expv[:, t, :], best[:, t, :], ACT.Exp, bias=negmax[:, t:t + 1],
                   accum_out=esum[:, t:t + 1]).then_inc(exp_ready, 1)

            def activate(u, t, g):
                i = t % NT
                cols = slice(g * GRP, (g + 1) * GRP)
                act.wait_ge(dots_done, u * TOPK + (g + 1) * GRP)
                if g == 0:
                    act.wait_ge(gates_ready, u + 1)
                fn(gel[:, i, cols], hid[:, i, cols], ACT.Gelu).then_inc(gel_ready, 1)
                act.wait_ge(gel_ready, u * NG + g + 1)
                for c in range(g * GRP, (g + 1) * GRP):
                    fn(actv[:, i, c:c + 1], gel[:, i, c:c + 1], ACT.Copy, scale=gates[:, i, c:c + 1])\
                        .then_inc(actv_ready, 1)
                for c in range(g * GRP, (g + 1) * GRP):
                    act.wait_ge(actv_ready, u * TOPK + c + 1)
                    act.wait_ge(slot_free, u * TOPK + c + 1 + RING - DIAGS)
                    fn(diag[:, c % DIAGS, :], ident[:, :], ACT.Copy, scale=actv[:, i, c:c + 1])\
                        .then_inc(diag_ready, 1)

            def keep_x2T(t):
                act.wait_ge(x2_tr, t + 1)
                fn(x1T[:, :, t * P:(t + 1) * P], psf[:, 3072:4096].rearrange("p (k n) -> p k n", k=KD),
                   ACT.Copy).then_inc(x2T_ready, 1)

            def gate_sigmoid(t, j):
                act.wait_ge(gate_in, 2 * t + j + 1)
                half = x1[:, t, j * HALF:(j + 1) * HALF]
                fn(half, half, ACT.Sigmoid).then_inc(gate_ready, 1)

            keep_query(0)
            keep_query(1)
            gate_exp(0, 0)

            def unit(h, t, last_head):
                u = h * NT + t
                for g in range(NG):
                    activate(u, t, g)
                    if g == 4 and not (last_head and t == NT - 1):
                        gate_exp(u + 1, (t + 1) % NT)
                    if g == 4 and not (last_head and t + 2 >= NT):
                        keep_query(u + 2)
                    if last_head and t and g == 2:
                        sqrt_var(1)
                    if last_head and t and g == 5:
                        keep_x2T(t - 1)
                if last_head and t:
                    gate_sigmoid(t - 1, 0)
                    gate_sigmoid(t - 1, 1)
                    sqrt_var(1)

            with act.Fori(0, PH - 1) as h:
                for t in range(NT):
                    unit(h, t, False)
            for t in range(NT):
                unit(PH - 1, t, True)
            sqrt_var(1)
            keep_x2T(NT - 1)
            gate_sigmoid(NT - 1, 0)
            gate_sigmoid(NT - 1, 1)
            sqrt_var(1)

        @block.vector
        def _(dve):
            v = nc.vector
            seen = Counter(dve_at)

            def step(ins):
                seen.inc(ins)
                dve.wait_ge(dve_at, seen.base + seen.n)

            def step_to_max(ins):
                seen.inc(ins)
                hold(dve, dve_at, seen.base + seen.n, dve_passed)

            asked = Counter(var_ready)

            def rsqrt(n, out_):
                dve.wait_ge(std_ready, asked.n)
                step(v.reciprocal(rinv[:, 0:n], std[:, 0:n]))
                step(v.tensor_tensor(rtmp[:, 0:n], rinv[:, 0:n], rinv[:, 0:n], ALU.mult))
                step(v.scalar_tensor_tensor(out=rtmp[:, 0:n], in0=rtmp[:, 0:n], scalar=-0.5, in1=var_e[:, 0:n],
                                            op0=ALU.mult, op1=ALU.mult))
                step(v.scalar_tensor_tensor(out=out_, in0=rtmp[:, 0:n], scalar=1.5, in1=rinv[:, 0:n],
                                            op0=ALU.add, op1=ALU.mult))

            def layer_norm_stats(src):
                for j in range(2):
                    step(v.bn_stats(stats[:, j, :], src[:, j * HALF:(j + 1) * HALF]))
                step(v.bn_aggr(aggr[:, 0, :], stats[:, 0:2, :]))
                asked.inc(v.tensor_scalar_add(var_e[:, 0:1], aggr[:, 0, 1:2], EPS))

            def layer_norm_apply(src, g, b, done):
                rsqrt(1, rstd[:, 0:1])
                step(v.tensor_scalar(src, src, aggr[:, 0, 0:1], rstd[:, 0:1], ALU.subtract, ALU.mult))
                step(v.tensor_tensor(src, src, g, ALU.mult))
                v.tensor_tensor(src, src, b, ALU.add).then_inc(done, 1)

            for b in range(WB):
                dve.wait_ge(proj_done, 4 + b + 1)
                v.tensor_copy(kT[:, b, :], ps[:, 4 + b, :]).then_inc(dve_evac, 1)
            for t in range(NT):
                dve.wait_ge(act_evac, 4 + t + 1)
                step(v.bn_stats(stats[:, t, :], gv[:, t, :]))
                step(v.bn_aggr(aggr[:, t, :], stats[:, t, :]))
            asked.inc(v.tensor_scalar_add(var_e[:, 0:NT], aggr[:, :, 1], EPS))
            for t in range(NT):
                dve.wait_ge(proj_done, 16 + t + 1)
                v.tensor_copy(v_tok[:, t, :], ps[:, t, :]).then_inc(dve_evac, 1)
            rsqrt(NT, rstd[:, 0:NT])
            dve.wait_ge(small_in, 16 * 7)

            def gv_norm(t):
                step(v.tensor_scalar(gv[:, t, :], gv[:, t, :], aggr[:, t, 0:1], rstd[:, t:t + 1],
                                     ALU.subtract, ALU.mult))
                step(v.tensor_tensor(gv[:, t, :], gv[:, t, :], vn_g, ALU.mult))
                i = v.tensor_tensor(gv[:, t, :], gv[:, t, :], vn_b, ALU.add)
                if t == NT - 1:
                    i.then_inc(gvn_ready, 1)

            def take_pair(b):
                dve.wait_ge(attn_sq, b + 1)
                v.tensor_scalar(attnT[:, b, :], ps[:, 6 + b % 2, :], gA[:, b:b + 1], None, ALU.mult)\
                    .then_inc(attn_scaled, 1)

            for h in range(AH):
                z = psf[:, (h % 2) * 1536:(h % 2) * 1536 + ZCOLS]
                if h % 2 == 0 and h < AH:
                    gv_norm(h // 2)
                dve.wait_ge(log_ready, h + 1)
                v.scalar_tensor_tensor(out=l_buf[:, h % 2, :], in0=z, scalar=0.0, in1=e_buf[:, h % 2, :],
                                       op0=ALU.max, op1=ALU.add).then_inc(l_ready, 1)
                if h % 2 == 1 and h >= 3:
                    take_pair(h // 2 - 1)
            take_pair(WB - 1)
            for b in range(WB):
                dve.wait_ge(mixed_done, b + 1)
                m = ps[:, b, :].rearrange("p (t n) -> p t n", t=NT)
                bias = bs_b[:, b, :].unsqueeze(1).to_broadcast([P, NT, P])
                dst = l_buf[:, b % 2, 0:S]
                step(v.tensor_tensor(dst.rearrange("p (t n) -> p t n", t=NT), m, bias, ALU.add))
                v.tensor_tensor(guT[:, b, :], dst, guT[:, b, :], ALU.mult).then_inc(gm_ready, 1)
            dve.wait_ge(ssq_done, 1)
            asked.inc(v.tensor_scalar(var_e[:, 0:2 * NT], ps[:, 4, 0:2 * NT], 1.0 / AW, EPS, ALU.mult, ALU.add))
            rsqrt(2 * NT, rsn[:, :])
            v.tensor_copy(rtmp[:, 0:1], rsn[:, 0:1]).then_inc(rms_ready, 1)
            dve.wait_ge(x_in, 16)
            dve.wait_ge(ln1_in, 32)
            for t in range(NT):
                xt = x1[:, t, :]
                dve.wait_ge(pa_scaled, t + 1)
                step(v.scalar_tensor_tensor(out=xt, in0=x_nat[:, t, :], scalar=ALPHA, in1=xt,
                                            op0=ALU.mult, op1=ALU.add))
                pg = psf[:, (t % 2) * 2048 + D:(t % 2) * 2048 + 2 * D]
                step(v.scalar_tensor_tensor(out=xt, in0=pg, scalar=rsn[:, NT + t:NT + t + 1], in1=xt,
                                            op0=ALU.mult, op1=ALU.add))
                layer_norm_stats(xt)
                layer_norm_apply(xt, ln1_g, ln1_b, x1_ready)

            dve.wait_ge(x1T_ready, NT)
            v.memset(acc, 0.0).then_inc(sum_free, 2)

            def rank_keys(u, half):
                if half == 0:
                    hold(dve, score_done, u + 1, dve_passed)
                if True:
                    s = ps[:, 5, half * NKEY:(half + 1) * NKEY]
                    step_to_max(v.max(out=top[:, half, 0:8], in_=s))
                    v.max_index(out=topi[:, half, 0:8], in_max=top[:, half, 0:8], in_values=s)
                    step_to_max(v.match_replace(out=left[:, half, :], in_to_replace=top[:, half, 0:8], in_values=s,
                                         imm_value=NEG))
                    step_to_max(v.max(out=top[:, half, 8:16], in_=left[:, half, :]))
                    k = v.max_index(out=topi[:, half, 8:16], in_max=top[:, half, 8:16], in_values=left[:, half, :])
                    if half == 0:
                        step_to_max(k)
                    else:
                        k.then_inc(score_used, 1)

            def rank_sums(u, t):
                i = t % NT
                first = top[:, 0, :].unsqueeze(2).to_broadcast([P, TOPK, TOPK])
                second = top[:, 1, :].unsqueeze(1).to_broadcast([P, TOPK, TOPK])
                step(v.tensor_tensor(cand[:, :].rearrange("p (x y) -> p x y", x=TOPK), first, second, ALU.add))
                dve.wait_ge(score_used, u + 1)
                step_to_max(v.tensor_copy(topf[:, :, :], topi[:, :, :]))
                step_to_max(v.max(out=best[:, i, 0:8], in_=cand[:, :]))
                v.max_index(out=besti[:, 0:8], in_max=best[:, i, 0:8], in_values=cand[:, :])
                step_to_max(v.match_replace(out=cleft[:, :], in_to_replace=best[:, i, 0:8], in_values=cand[:, :],
                                     imm_value=NEG))
                step_to_max(v.max(out=best[:, i, 8:16], in_=cleft[:, :]))
                step(v.max_index(out=besti[:, 8:16], in_max=best[:, i, 8:16], in_values=cleft[:, :]))

            def rank_ids(u, t):
                i = t % NT
                v.tensor_scalar(negmax[:, i:i + 1], best[:, i, 0:1], -1.0, None, ALU.mult)
                v.tensor_scalar(nib[:, 0, :], besti[:, :], 4, None, ALU.logical_shift_right)
                step(v.tensor_scalar(nib[:, 1, :], besti[:, :], 15, None, ALU.bitwise_and))
                step(v.tensor_copy(nibf[:, :, :], nib[:, :, :]))
                want = nibf[:, :, :].unsqueeze(3).to_broadcast([P, 2, TOPK, TOPK])
                lanes = iota16[:, :].unsqueeze(1).unsqueeze(1).to_broadcast([P, 2, TOPK, TOPK])
                vals = topf[:, :, :].unsqueeze(2).to_broadcast([P, 2, TOPK, TOPK])
                step(v.tensor_tensor(hot[:, :, :, :], lanes, want, ALU.is_equal))
                step(v.tensor_tensor(hot[:, :, :, :], hot[:, :, :, :], vals, ALU.mult))
                step(v.reduce_sum(pick[:, :, :], hot[:, :, :, :], AX.X))
                v.scalar_tensor_tensor(out=ids[:, i, :], in0=pick[:, 0, :], scalar=float(NKEY), in1=pick[:, 1, :],
                                       op0=ALU.mult, op1=ALU.add).then_inc(ids_ready, 1)

            def norm_gates(u, t):
                i = t % NT
                dve.wait_ge(exp_ready, u + 1)
                step(v.reciprocal(erec[:, i:i + 1], esum[:, i:i + 1]))
                v.tensor_scalar(gates[:, i, :], expv[:, i, :], erec[:, i:i + 1], None, ALU.mult)\
                    .then_inc(gates_ready, 1)

            def dots(u, t, g):
                for c in range(g * GRP, (g + 1) * GRP):
                    r = rows[:, c % RING, 0:D]
                    dve.wait_ge(rows_in[c % RING], u * (16 * TOPK // RING) + 16 * (c // RING + 1))
                    v.tensor_tensor_reduce(out=r, in0=r, in1=x1[:, t, :], scale=1.0, scalar=0.0,
                                           op0=ALU.mult, op1=ALU.add,
                                           accum_out=hid[:, t, c:c + 1]).then_inc(dots_done, 1)

            def add_unit(u, t):
                dve.wait_ge(slot_free, u * TOPK + TOPK + RING)
                b = 2 * (t % 2) * 512
                v.tensor_tensor(acc[:, t % NT, :], psf[:, b:b + D], acc[:, t % NT, :], ALU.add)\
                    .then_inc(sum_free, 1)

            def x2_stats(t):
                dve.wait_ge(sum_free, 2 + NT * PH - NT + t + 1)
                if t == 0:
                    dve.wait_ge(tail_in, 16 * 8)
                step(v.scalar_tensor_tensor(out=acc[:, t, :], in0=x1[:, t, :], scalar=ALPHA, in1=acc[:, t, :],
                                            op0=ALU.mult, op1=ALU.add))
                layer_norm_stats(acc[:, t, :])

            def ple_half(t, j):
                half = x1[:, t, j * HALF:(j + 1) * HALF]
                cols = slice(j * HALF, (j + 1) * HALF)
                dve.wait_ge(ple_done, 2 * t + j + 1)
                v.tensor_tensor(half, ps[:, 6, :], b_gate[:, cols], ALU.add).then_inc(gate_in, 1)
                dve.wait_ge(gate_ready, 2 * t + j + 1)
                v.tensor_tensor(half, ps[:, 7, :], half, ALU.mult).then_inc(ple_used, 1)
                dve.wait_ge(ple_used, 2 * t + j + 1)
                step(v.scalar_tensor_tensor(out=acc[:, t, cols], in0=acc[:, t, cols], scalar=ALPHA, in1=half,
                                            op0=ALU.mult, op1=ALU.add))

            def finish(t):
                ple_half(t, 0)
                ple_half(t, 1)
                layer_norm_stats(acc[:, t, :])
                layer_norm_apply(acc[:, t, :], ln3_g, ln3_b, out_ready)

            for half in range(2):
                rank_keys(0, half)
            rank_sums(0, 0)
            rank_ids(0, 0)
            norm_gates(0, 0)

            def unit(h, t, last_head, first_unit=False):
                u = h * NT + t
                more = not (last_head and t == NT - 1)
                for g in range(NG):
                    dots(u, t, g)
                    if more and g in (0, 1):
                        rank_keys(u + 1, g)
                    if more and g == 2:
                        rank_sums(u + 1, t + 1)
                    if more and g == 3:
                        rank_ids(u + 1, t + 1)
                    if g == 1 and t:
                        add_unit(u - 1, t - 1)
                        if last_head:
                            x2_stats(t - 1)
                    if g == 2 and last_head and t:
                        layer_norm_apply(acc[:, t - 1, :], ln2_g, ln2_b, x2_ready)
                    if more and g == 5:
                        norm_gates(u + 1, t + 1)
                if last_head and t:
                    finish(t - 1)
                if t == NT - 1:
                    add_unit(u, t)

            before = seen.n
            with dve.Fori(0, PH - 1) as h:
                seen.base, seen.n = h * HEAD_STEPS + before, 0
                for t in range(NT):
                    unit(h, t, False)
                assert seen.n == HEAD_STEPS
            seen.base, seen.n = 0, before + HEAD_STEPS * (PH - 1)
            for t in range(NT):
                unit(PH - 1, t, True)
            x2_stats(NT - 1)
            layer_norm_apply(acc[:, NT - 1, :], ln2_g, ln2_b, x2_ready)
            finish(NT - 1)


def kernel(**inputs):
    import concourse.bacc as _bacc
    from concourse.bass_utils import run_bass_kernel_spmd as _run

    f = {k: np.asarray(x) for k, x in inputs.items()}

    def chunks(w):
        return w.reshape(-1, P, w.shape[-1]).transpose(1, 0, 2)

    def blocks(w):
        return w.reshape(KD, P, WB, P).transpose(1, 2, 0, 3).reshape(P, -1)

    w = f["w_in"][0]
    x = f["x"][0]
    arrays = {
        "xT": chunks(x.T),
        "x": x.reshape(NT, P, D).transpose(1, 0, 2),
        "w_q": blocks(w[:, 0:AW]),
        "w_k": blocks(w[:, AW:2 * AW]),
        "w_v": chunks(w[:, 2 * AW:3 * AW]).reshape(P, -1),
        "w_gu": blocks(w[:, 3 * AW:4 * AW]),
        "w_gv": chunks(w[:, 4 * AW:5 * AW]).reshape(P, -1),
        "wsT": f["gmlp_ws"][0].transpose(2, 0, 1),
        "gA": f["attn_out_g"][0].reshape(WB, P).T,
        "gG": f["gmlp_out_g"][0].reshape(WB, P).T,
        "w_out": chunks(f["w_out"][0]),
        "wq": f["peer_wq"][0].reshape(KD, P, PH, QD).transpose(2, 1, 0, 3),
        "subk": f["peer_subkeys"][0].transpose(3, 0, 1, 2).reshape(P, -1),
        "uv": np.concatenate([f["peer_u"][0], f["peer_v"][0]], axis=1),
        "w_gate": chunks(f["ple_wgate"][0]),
        "w_proj": chunks(f["ple_wproj"][0]),
        "pT": chunks(f["p"][0, 0].T),
    }
    for name in ("gmlp_vn_g", "gmlp_vn_b", "gmlp_bs", "ln1_g", "ln1_b", "ln2_g", "ln2_b", "ln3_g", "ln3_b",
                 "ple_bgate"):
        arrays[name] = f[name]
    nc = _bacc.Bacc("TRN2", target_bir_lowering=False, num_devices=1)
    data, aps = {}, {}
    for name, array in arrays.items():
        data[f"in_{name}"] = np.ascontiguousarray(array)
        aps[name] = nc.dram_tensor(f"in_{name}", array.shape, FP32, kind="ExternalInput").ap()
    out = nc.dram_tensor("out_0", (1, S, D), FP32, kind="ExternalOutput").ap()
    build(nc, aps, out)
    return _run(nc, [data], core_ids=[0]).results[0]["out_0"]
```

```python
import math
from contextlib import ExitStack

import numpy as np
import concourse.bass as bass
from concourse import mybir

FP32 = mybir.dt.float32
U32 = mybir.dt.uint32
I32 = mybir.dt.int32
ALU = mybir.AluOpType
ACT = mybir.ActivationFunctionType
AX = mybir.AxisListType

P = 128
D = 1024
S = 512
NT = S // P
KD = D // P
AH, DH = 8, 64
AW = AH * DH
G = 8
WB = AW // P
PH, TOPK, NKEY = 8, 16, 128
QD = 256
PLE = 256
EPS = 1e-5
ALPHA = 2.0 ** 0.25
QSCALE = 1.0 / math.sqrt(DH)
NEG = -3.0e38
ARENA = 37632

RING = 8
GRP = 2
NG = TOPK // GRP
RANK_STEPS = 18
HEAD_STEPS = NT * (RANK_STEPS + 1)
DIAGS = 4
HALF = D // 2

ZOFF = {0: 0, 1: 512, 3: 896, 2: 1024}
ZCOLS = 1280


def zlen(s):
    return S - P * s


class Counter:

    def __init__(self, sem):
        self.sem, self.n, self.base = sem, 0, 0

    def inc(self, instruction, by=1):
        instruction.then_inc(self.sem, by)
        self.n += by


def hold(eng, sem, value, passed):
    eng.wait_ge(sem, value)
    eng.sem_inc(passed, 1)


def build(nc, a, out):
    ctx = ExitStack()
    with ctx:
        def sb(name, shape, dt=FP32):
            return ctx.enter_context(nc.sbuf_tensor(name, shape, dt))

        def sem(name):
            return ctx.enter_context(nc.semaphore(name))

        x1 = sb("x1", [P, NT, D])
        x1T = sb("x1T", [P, KD, S])
        wq_head = sb("wq_head", [P, KD, QD])
        subk = sb("subk", [P, PH * 2 * NKEY])
        ident = sb("ident", [P, P])
        neg_tri = sb("neg_tri", [P, P])
        neg_one = sb("neg_one", [P, P])
        ones = sb("ones", [P, 1])
        iota16 = sb("iota16", [P, TOPK])
        gA = sb("gA", [P, WB])
        gG = sb("gG", [P, WB])
        stats = sb("stats", [P, 4, 6])
        aggr = sb("aggr", [P, 4, 2])
        var_e = sb("var_e", [P, 8])
        std = sb("std", [P, 8])
        rinv = sb("rinv", [P, 8])
        rtmp = sb("rtmp", [P, 8])
        rstd = sb("rstd", [P, 8])
        rsn = sb("rsn", [P, 2 * NT])

        arena = sb("arena", [P, ARENA])
        at = [0]

        def take(n):
            at[0] += n
            return arena[:, at[0] - n:at[0]]

        ring_w = take(8192)
        wgrp = [ring_w[:, 0:4096], ring_w[:, 4096:8192]]
        w_out = ring_w.rearrange("p (c n) -> p c n", c=8)
        ln1_g, ln1_b = take(D), take(D)
        qk_flat = take(4096)
        qT = qk_flat[:, 0:2048].rearrange("p (b s) -> p b s", b=WB)
        kT = qk_flat[:, 2048:4096].rearrange("p (b s) -> p b s", b=WB)
        x_nat = qk_flat.rearrange("p (t d) -> p t d", t=NT)
        attnT = take(2048).rearrange("p (b s) -> p b s", b=WB)
        gmT = take(2048).rearrange("p (b s) -> p b s", b=WB)
        live = at[0]
        xT_flat = take(4096)
        xT = xT_flat.rearrange("p (k s) -> p k s", k=KD)
        squares = xT_flat.rearrange("p (c s) -> p c s", c=8)
        guT = take(2048).rearrange("p (b s) -> p b s", b=WB)
        v_tok = take(2048).rearrange("p (t c) -> p t c", t=NT)
        gv = take(2048).rearrange("p (t c) -> p t c", t=NT)
        wsT = take(1024).rearrange("p (g t) -> p g t", g=G)
        vn_g, vn_b = take(AW), take(AW)
        bs_b = take(AW).rearrange("p (b t) -> p b t", b=WB)
        e_buf = take(3 * ZCOLS).rearrange("p (i n) -> p i n", i=3)
        l_buf = take(2 * ZCOLS).rearrange("p (i n) -> p i n", i=2)
        dead = at[0]

        at[0] = live
        rows = take(RING * 2 * D).rearrange("p (r n) -> p r n", r=RING)
        assert at[0] <= dead
        pT = take(2 * S).rearrange("p (k s) -> p k s", k=2)
        b_gate = take(D)
        assert at[0] <= ARENA
        at[0] = 0
        acc = take(NT * D).rearrange("p (t d) -> p t d", t=NT)
        w_gate = take(KD * D).rearrange("p (k n) -> p k n", k=KD)
        w_proj = take(2 * D).rearrange("p (k n) -> p k n", k=2)
        ln2_g, ln2_b, ln3_g, ln3_b = (take(D) for _ in range(4))
        assert at[0] <= live

        qs = sb("qs", [P, QD])
        left = sb("left", [P, 2, NKEY])
        top = sb("top", [P, 2, TOPK])
        topi = sb("topi", [P, 2, TOPK], U32)
        topf = sb("topf", [P, 2, TOPK])
        cand = sb("cand", [P, TOPK * TOPK])
        cleft = sb("cleft", [P, TOPK * TOPK])
        best = sb("best", [P, NT, TOPK])
        besti = sb("besti", [P, TOPK], U32)
        nib = sb("nib", [P, 2, TOPK], U32)
        nibf = sb("nibf", [P, 2, TOPK])
        hot = sb("hot", [P, 2, TOPK, TOPK])
        pick = sb("pick", [P, 2, TOPK])
        ids = sb("ids", [P, NT, TOPK], I32)
        negmax = sb("negmax", [P, NT])
        expv = sb("expv", [P, NT, TOPK])
        esum = sb("esum", [P, NT])
        erec = sb("erec", [P, NT])
        gates = sb("gates", [P, NT, TOPK])
        hid = sb("hid", [P, NT, TOPK])
        gel = sb("gel", [P, NT, TOPK])
        actv = sb("actv", [P, NT, TOPK])
        diag = sb("diag", [P, DIAGS, P])

        ps = ctx.enter_context(nc.psum_tensor("ps", [P, 8, 512], FP32))
        psf = ps[:, :, :].rearrange("p b n -> p (b n)")

        xT_in = sem("xT_in")
        w_in = [sem(f"w_in{i}") for i in range(8)]
        small_in = sem("small_in")
        wout_in = [sem("wout_in0"), sem("wout_in1")]
        x_in = sem("x_in")
        ln1_in = sem("ln1_in")
        subk_in = sem("subk_in")
        wq_in = sem("wq_in")
        tail_in = sem("tail_in")
        const_ready = sem("const_ready")
        ws_masked = sem("ws_masked")
        proj_done = sem("proj_done")
        act_evac = sem("act_evac")
        dve_evac = sem("dve_evac")
        z_done = sem("z_done")
        log_ready = sem("log_ready")
        l_ready = sem("l_ready")
        l_masked = sem("l_masked")
        arg_done = sem("arg_done")
        a_ready = sem("a_ready")
        a_masked = sem("a_masked")
        av_done = sem("av_done")
        attn_sq = sem("attn_sq")
        attn_scaled = sem("attn_scaled")
        gvn_ready = sem("gvn_ready")
        mixed_done = sem("mixed_done")
        gm_ready = sem("gm_ready")
        gm_out = sem("gm_out")
        ssq_done = sem("ssq_done")
        rms_ready = sem("rms_ready")
        pa_done = sem("pa_done")
        pg_done = sem("pg_done")
        pa_scaled = sem("pa_scaled")
        x1_ready = sem("x1_ready")
        x1_tr = sem("x1_tr")
        x1T_ready = sem("x1T_ready")
        var_ready = sem("var_ready")
        std_ready = sem("std_ready")
        dve_at = sem("dve_at")
        act_at = sem("act_at")

        q_done = sem("q_done")
        qs_ready = sem("qs_ready")
        score_done = sem("score_done")
        score_used = sem("score_used")
        ids_ready = sem("ids_ready")
        exp_ready = sem("exp_ready")
        gates_ready = sem("gates_ready")
        rows_in = [sem(f"rows_in{i}") for i in range(RING)]
        dots_done = sem("dots_done")
        gel_ready = sem("gel_ready")
        actv_ready = sem("actv_ready")
        diag_ready = sem("diag_ready")
        slot_free = sem("slot_free")
        sum_free = sem("sum_free")
        x2_ready = sem("x2_ready")
        x2_tr = sem("x2_tr")
        x2T_ready = sem("x2T_ready")
        ple_done = sem("ple_done")
        gate_in = sem("gate_in")
        gate_ready = sem("gate_ready")
        ple_used = sem("ple_used")
        out_ready = sem("out_ready")
        out_done = sem("out_done")
        dve_passed = sem("dve_passed")
        pool_passed = sem("pool_passed")

        block = ctx.enter_context(nc.Block())

        @block.sync
        def _(sp):
            sp.dma_start(xT, a["xT"][:, :, :]).then_inc(xT_in, 16)
            for b in range(WB):
                sp.dma_start(wgrp[0][:, b * D:(b + 1) * D],
                             a["w_q"][:, b * D:(b + 1) * D]).then_inc(w_in[b], 16)
            sp.dma_start(wgrp[1], a["w_k"][:, :]).then_inc(w_in[4], 16)
            sp.dma_start(wsT, a["wsT"][:, :, :]).then_inc(small_in, 16)
            sp.dma_start(vn_g, a["gmlp_vn_g"][0, :].partition_broadcast(P)).then_inc(small_in, 16)
            sp.dma_start(vn_b, a["gmlp_vn_b"][0, :].partition_broadcast(P)).then_inc(small_in, 16)
            for half in range(2):
                sp.dma_start(bs_b[half * DH:(half + 1) * DH, :, :],
                             a["gmlp_bs"][0].rearrange("(b h) t -> h b t", h=2)[half]
                             .partition_broadcast(DH)).then_inc(small_in, 16)
            sp.dma_start(gA[:, :], a["gA"][:, :]).then_inc(small_in, 16)
            sp.dma_start(gG[:, :], a["gG"][:, :]).then_inc(small_in, 16)
            sp.dma_start(subk[:, :], a["subk"][:, :]).then_inc(subk_in, 16)
            sp.dma_start(wq_head[:, :, :], a["wq"][0]).then_inc(wq_in, 16)
            sp.wait_ge(proj_done, 4)
            sp.dma_start(wgrp[0], a["w_v"][:, :]).then_inc(w_in[5], 16)
            sp.wait_ge(proj_done, 8)
            sp.dma_start(wgrp[1], a["w_gv"][:, :]).then_inc(w_in[6], 16)
            sp.wait_ge(proj_done, 12)
            sp.dma_start(wgrp[0], a["w_gu"][:, :]).then_inc(w_in[7], 16)
            sp.dma_start(ln1_g, a["ln1_g"][0, :].partition_broadcast(P)).then_inc(ln1_in, 16)
            sp.dma_start(ln1_b, a["ln1_b"][0, :].partition_broadcast(P)).then_inc(ln1_in, 16)
            sp.wait_ge(proj_done, 16)
            sp.dma_start(w_out[:, 4:8, :], a["w_out"][:, 4:8, :]).then_inc(wout_in[1], 16)
            sp.wait_ge(proj_done, 20)
            sp.dma_start(w_out[:, 0:4, :], a["w_out"][:, 0:4, :]).then_inc(wout_in[0], 16)
            sp.wait_ge(arg_done, AH)
            sp.dma_start(x_nat, a["x"][:, :, :]).then_inc(x_in, 16)
            sp.wait_ge(x1T_ready, NT)
            for dst, src in ((w_gate, a["w_gate"][:, :, :]), (w_proj, a["w_proj"][:, :, :]), (pT, a["pT"][:, :, :])):
                sp.dma_start(dst, src).then_inc(tail_in, 16)
            for dst, name in ((ln2_g, "ln2_g"), (ln2_b, "ln2_b"), (ln3_g, "ln3_g"), (ln3_b, "ln3_b"),
                              (b_gate, "ple_bgate")):
                sp.dma_start(dst, a[name][0, :].partition_broadcast(P)).then_inc(tail_in, 16)
            with sp.Fori(0, PH - 1) as h:
                sp.wait_ge(q_done, h * NT + NT)
                sp.dma_start(wq_head[:, :, :], a["wq"][bass.ds(h + 1, 1)].rearrange("h p k n -> (h p) k n"))\
                  .then_inc(wq_in, 16)
            for t in range(NT):
                sp.wait_ge(out_ready, t + 1)
                sp.dma_start(out[0, t * P:(t + 1) * P, :], acc[:, t, :]).then_inc(out_done, 16)
            sp.wait_ge(out_done, 16 * NT)

        @block.gpsimd
        def _(pool):
            nc.gpsimd.memset(ident[:, :], 0.0).then_inc(const_ready, 1)
            nc.gpsimd.memset(neg_tri[:, :], -1.0).then_inc(const_ready, 1)
            nc.gpsimd.memset(neg_one[:, :], -1.0).then_inc(const_ready, 1)
            nc.gpsimd.memset(ones[:, :], 1.0).then_inc(const_ready, 1)
            nc.gpsimd.iota(iota16[:, :], pattern=[[1, TOPK]], base=0, channel_multiplier=0,
                           allow_small_or_imprecise_dtypes=True).then_inc(const_ready, 1)
            pool.wait_ge(const_ready, 5)
            nc.gpsimd.affine_select(out=ident[:, :], in_=ident[:, :], compare_op=ALU.not_equal, fill=1.0,
                                    base=0, pattern=[[-1, P]], channel_multiplier=1).then_inc(const_ready, 1)
            nc.gpsimd.affine_select(out=neg_tri[:, :], in_=neg_tri[:, :], compare_op=ALU.is_ge, fill=0.0,
                                    base=0, pattern=[[-1, P]], channel_multiplier=1).then_inc(const_ready, 1)
            pool.wait_ge(small_in, 16 * 7)
            nc.gpsimd.affine_select(out=wsT, in_=wsT, compare_op=ALU.is_ge, fill=0.0, base=0,
                                    pattern=[[0, G], [1, P]], channel_multiplier=-1).then_inc(ws_masked, 1)

            def keep_past(buf, s, done):
                blk = buf[:, ZOFF[s]:ZOFF[s] + P]
                nc.gpsimd.affine_select(out=blk, in_=blk, compare_op=ALU.is_gt, fill=0.0, base=0,
                                        pattern=[[1, P]], channel_multiplier=-1).then_inc(done, 1)

            for h in range(AH + 1):
                if h < AH:
                    pool.wait_ge(l_ready, h + 1)
                    for s in range(NT):
                        keep_past(l_buf[:, h % 2, :], s, l_masked)
                if h >= 1:
                    pool.wait_ge(a_ready, h)
                    for s in range(NT):
                        keep_past(e_buf[:, (h - 1) % 3, :], s, a_masked)

            def gather_unit(u, t):
                pool.wait_ge(ids_ready, u + 1)
                for c in range(TOPK):
                    hold(pool, slot_free, u * TOPK + c + 1, pool_passed)
                    nc.gpsimd.indirect_dma_start(
                        out=rows[:, c % RING, :], out_offset=None, in_=a["uv"][:, :],
                        in_offset=bass.IndirectOffsetOnAxis(ap=ids[:, t, c:c + 1], axis=0),
                    ).then_inc(rows_in[c % RING], 16)

            with pool.Fori(0, PH) as h:
                for t in range(NT):
                    gather_unit(h * NT + t, t)

        @block.tensor
        def _(pe):
            mm = nc.tensor.matmul

            def project_T(bank, w, j):
                for k in range(KD):
                    i = mm(ps[:, bank, :], w[:, j * D + k * P:j * D + (k + 1) * P], xT[:, k, :],
                           start=(k == 0), stop=(k == KD - 1))
                i.then_inc(proj_done, 1)

            def project_tok(bank, w, t):
                for k in range(KD):
                    i = mm(ps[:, bank, :], xT[:, k, t * P:(t + 1) * P], w[:, k * AW:(k + 1) * AW],
                           start=(k == 0), stop=(k == KD - 1))
                i.then_inc(proj_done, 1)

            pe.wait_ge(xT_in, 16)
            for b in range(WB):
                pe.wait_ge(w_in[b], 16)
                project_T(b, wgrp[0], b)
            pe.wait_ge(w_in[4], 16)
            for b in range(WB):
                project_T(4 + b, wgrp[1], b)
            pe.wait_ge(w_in[5], 16)
            for t in range(NT):
                pe.wait_ge(act_evac, t + 1)
                project_tok(t, wgrp[0], t)
            pe.wait_ge(w_in[6], 16)
            for t in range(NT):
                pe.wait_ge(dve_evac, t + 1)
                project_tok(4 + t, wgrp[1], t)

            def z_cols(h, s, n0=0):
                base = (h % 2) * 3 * 512 + ZOFF[s]
                return psf[:, base + n0:base + zlen(s)]

            def scores(h, s, start):
                r = slice(DH * (h % 2), DH * (h % 2) + DH)
                return mm(z_cols(h, s), kT[r, h // 2, s * P:(s + 1) * P], qT[r, h // 2, s * P:S],
                          start=start, stop=False, skip_group_check=True)

            def open_scores(h):
                if h >= 2:
                    pe.wait_ge(a_ready, h - 1)
                for s in (0, 1, 3, 2):
                    i = scores(h, s, s != 3)
                i.then_inc(z_done, 1)

            def subtract_sums(h):
                pe.wait_ge(l_masked, NT * (h + 1))
                for s in (0, 1, 3, 2):
                    for j in range(s, NT):
                        n0 = (j - s) * P
                        i = mm(z_cols(h, s, n0), (neg_tri if j == s else neg_one)[:, :],
                               l_buf[:, h % 2, ZOFF[j]:ZOFF[j] + zlen(j)], start=False,
                               stop=(j == NT - 1), skip_group_check=True)
                i.then_inc(arg_done, 1)

            def weigh_values(h):
                pe.wait_ge(a_masked, NT * (h + 1))
                if h >= 4 and h % 2 == 0:
                    pe.wait_ge(attn_sq, h // 2 - 1)
                    pe.wait_ge(attn_scaled, h // 2 - 1)
                r = slice(DH * (h % 2), DH * (h % 2) + DH)
                for s in range(NT):
                    i = mm(ps[r, 6 + (h // 2) % 2, s * P:S], v_tok[:, s, h * DH:(h + 1) * DH],
                           e_buf[:, h % 3, ZOFF[s]:ZOFF[s] + zlen(s)], start=(s == 0), stop=(s == NT - 1),
                           skip_group_check=True)
                i.then_inc(av_done, 1)

            pe.wait_ge(const_ready, 7)
            pe.wait_ge(dve_evac, 7)
            open_scores(0)
            pe.wait_ge(w_in[7], 16)
            pe.wait_ge(dve_evac, 8)
            project_T(3, wgrp[0], 0)
            for b in range(1, WB):
                pe.wait_ge(act_evac, 4 + b)
                project_T(3 + b, wgrp[0], b)
            pe.wait_ge(act_evac, 4 + NT + WB)
            for h in range(AH + 1):
                if h + 1 < AH:
                    open_scores(h + 1)
                if h < AH:
                    subtract_sums(h)
                if h >= 1:
                    weigh_values(h - 1)

            pe.wait_ge(ws_masked, 1)
            pe.wait_ge(gvn_ready, 1)
            for b in range(WB):
                for g in (2 * b, 2 * b + 1):
                    r = slice(DH * (g % 2), DH * (g % 2) + DH)
                    for t in range(NT):
                        i = mm(ps[r, b, t * P:(t + 1) * P], gv[:, t, g * DH:(g + 1) * DH], wsT[:, g, :],
                               start=(t == 0), stop=True, skip_group_check=True)
                i.then_inc(mixed_done, 1)

            def sum_squares(kind):
                for t in range(NT):
                    for c in range(WB):
                        i = mm(ps[:, 4, kind * NT + t:kind * NT + t + 1],
                               squares[:, kind * WB + c, t * P:(t + 1) * P], ones[:, :],
                               start=(c == 0), stop=(c == WB - 1))
                if kind == 1:
                    i.then_inc(ssq_done, 1)

            def project_out(kind, t):
                src = (attnT, gmT)[kind]
                first_bank = (4 * (t % 2), 2)[kind]
                for j in range(2):
                    for c in range(WB):
                        i = mm(ps[:, first_bank + j, :], src[:, c, t * P:(t + 1) * P],
                               w_out[:, kind * WB + c, j * HALF:(j + 1) * HALF],
                               start=(c == 0), stop=(c == WB - 1))
                i.then_inc((pa_done, pg_done)[kind], 1)

            def transpose_x1(t):
                pe.wait_ge(x1_ready, t + 1)
                for k in range(KD):
                    i = nc.tensor.transpose(ps[:, (t % 2) * 4 + k // 4, (k % 4) * P:(k % 4 + 1) * P],
                                            x1[:, t, k * P:(k + 1) * P], ident[:, :])
                i.then_inc(x1_tr, 1)

            def query(h, t, u):
                if t == 0:
                    pe.wait_ge(wq_in, h * 16 + 16)
                pe.wait_ge(qs_ready, u)
                for half in range(2):
                    for k in range(KD):
                        i = mm(ps[:, 6, half * P:(half + 1) * P], wq_head[:, k, half * P:(half + 1) * P],
                               x1T[:, k, t * P:(t + 1) * P], start=(k == 0), stop=(k == KD - 1))
                i.then_inc(q_done, 1)

            def key_scores(h, t, u):
                pe.wait_ge(qs_ready, u + 1)
                pe.wait_ge(score_used, u)
                for half in range(2):
                    i = mm(ps[:, 7, half * P:(half + 1) * P], qs[:, half * P:(half + 1) * P],
                           subk[:, bass.ds((h * 2 + half) * NKEY, NKEY)], start=True, stop=True)
                i.then_inc(score_done, 1)

            def combine(u, t, c):
                if c == 0:
                    pe.wait_ge(sum_free, u + 1)
                pe.wait_ge(diag_ready, u * TOPK + c + 1)
                for j in range(2):
                    i = mm(ps[:, 2 * (t % 2) + j, :], diag[:, c % DIAGS, :],
                           rows[:, c % RING, D + j * HALF:D + (j + 1) * HALF],
                           start=(c == 0), stop=(c == TOPK - 1))
                i.then_inc(slot_free, 1)

            def x2_transposes(t):
                pe.wait_ge(x2_ready, t + 1)
                if t:
                    pe.wait_ge(ple_used, 2 * t)
                for k in range(KD):
                    i = nc.tensor.transpose(ps[:, 4 + k // 4, (k % 4) * P:(k % 4 + 1) * P],
                                            acc[:, t, k * P:(k + 1) * P], ident[:, :])
                i.then_inc(x2_tr, 1)

            def ple_products(t, j):
                if t == 0 and j == 0:
                    pe.wait_ge(tail_in, 16 * 8)
                if j == 0:
                    pe.wait_ge(x2T_ready, t + 1)
                else:
                    pe.wait_ge(ple_used, 2 * t + 1)
                for k in range(KD):
                    mm(ps[:, 4, :], x1T[:, k, t * P:(t + 1) * P], w_gate[:, k, j * HALF:(j + 1) * HALF],
                       start=(k == 0), stop=(k == KD - 1))
                for k in range(2):
                    i = mm(ps[:, 5, :], pT[:, k, t * P:(t + 1) * P], w_proj[:, k, j * HALF:(j + 1) * HALF],
                           start=(k == 0), stop=(k == 1))
                i.then_inc(ple_done, 1)

            pe.wait_ge(wout_in[0], 16)
            pe.wait_ge(wout_in[1], 16)
            pe.wait_ge(attn_scaled, WB)
            pe.wait_ge(gm_ready, 2)
            project_out(0, 0)
            pe.wait_ge(attn_sq, WB)
            sum_squares(0)
            pe.wait_ge(gm_out, WB)
            sum_squares(1)
            project_out(1, 0)
            nc.tensor.matmul(ps[:, 5, 0:1], ident[:, :], ones[:, :], start=True, stop=True)\
              .then_inc(slot_free, RING)
            pe.wait_ge(rms_ready, 1)
            project_out(0, 1)
            pe.wait_ge(subk_in, 16)
            for t in range(NT):
                transpose_x1(t)
                if t < 2:
                    pe.wait_ge(x1T_ready, t + 1)
                    query(0, t, t)
                    key_scores(0, t, t)
                if t + 1 < NT:
                    project_out(1, t + 1)
                if t + 2 < NT:
                    pe.wait_ge(x1T_ready, t + 1)
                    project_out(0, t + 2)
            pe.wait_ge(x1T_ready, NT)

            def unit(h, t, last_head):
                u = h * NT + t
                ahead = (h, t + 2, u + 2) if t + 2 < NT else (h + 1, t + 2 - NT, u + 2)
                more = not (last_head and t + 2 >= NT)
                for c in range(TOPK):
                    combine(u, t, c)
                    if c == 9 and more:
                        query(*ahead)
                    if c == 11 and more:
                        key_scores(*ahead)
                    if last_head and t:
                        if c == 7:
                            x2_transposes(t - 1)
                        if c == 11:
                            ple_products(t - 1, 0)
                        if c == 15:
                            ple_products(t - 1, 1)

            with pe.Fori(0, PH - 1) as h:
                for t in range(NT):
                    unit(h, t, False)
            for t in range(NT):
                unit(PH - 1, t, True)
            x2_transposes(NT - 1)
            ple_products(NT - 1, 0)
            ple_products(NT - 1, 1)

        @block.scalar
        def _(act):
            fn = nc.scalar.activation
            for b in range(WB):
                act.wait_ge(proj_done, b + 1)
                fn(qT[:, b, :], ps[:, b, :], ACT.Copy, scale=QSCALE).then_inc(act_evac, 1)
            for t in range(NT):
                act.wait_ge(proj_done, 12 + t + 1)
                fn(gv[:, t, :], ps[:, 4 + t, :], ACT.Gelu).then_inc(act_evac, 1)
            stds = Counter(std_ready)

            def sqrt_var(n):
                act.wait_ge(var_ready, stds.n + 1)
                stds.inc(fn(std[:, 0:n], var_e[:, 0:n], ACT.Sqrt))

            def log_terms(h):
                e = e_buf[:, h % 3, :]
                act.wait_ge(z_done, h + 1)
                if h >= 3:
                    act.wait_ge(av_done, h - 2)
                fn(e, psf[:, (h % 2) * 1536:(h % 2) * 1536 + ZCOLS], ACT.Abs).then_inc(act_at, 1)
                act.wait_ge(act_at, 2 * h + 1)
                fn(e, e, ACT.Exp, scale=-1.0).then_inc(act_at, 1)
                act.wait_ge(act_at, 2 * h + 2)
                fn(e, e, ACT.Ln, bias=1.0).then_inc(log_ready, 1)

            act.preload_act_table_set("natural_log_exp_and_others")
            log_terms(0)
            for b in range(WB):
                act.wait_ge(proj_done, 16 + b + 1)
                fn(guT[:, b, :], ps[:, 3 + b, :], ACT.Gelu).then_inc(act_evac, 1)
            sqrt_var(NT)
            act.preload_act_table_set("natural_log_exp_and_others")
            for h in range(1, AH + 1):
                if h < AH:
                    log_terms(h)
                g = h - 1
                act.wait_ge(arg_done, g + 1)
                fn(e_buf[:, g % 3, :], psf[:, (g % 2) * 1536:(g % 2) * 1536 + ZCOLS], ACT.Exp)\
                    .then_inc(a_ready, 1)
                if g % 2 == 0 and g >= 2:
                    b = g // 2 - 1
                    act.wait_ge(av_done, g)
                    fn(squares[:, b, :], ps[:, 6 + b % 2, :], ACT.Square).then_inc(attn_sq, 1)
            act.wait_ge(av_done, AH)
            fn(squares[:, WB - 1, :], ps[:, 6 + (WB - 1) % 2, :], ACT.Square).then_inc(attn_sq, 1)
            for b in range(WB):
                act.wait_ge(gm_ready, b + 1)
                fn(squares[:, WB + b, :], guT[:, b, :], ACT.Square)
                fn(gmT[:, b, :], guT[:, b, :], ACT.Copy, scale=gG[:, b:b + 1]).then_inc(gm_out, 1)
            sqrt_var(2 * NT)

            def scaled_attn(t):
                act.wait_ge(pa_done, t + 1)
                act.wait_ge(rms_ready, 1)
                fn(x1[:, t, :], psf[:, (t % 2) * 2048:(t % 2) * 2048 + D], ACT.Copy,
                   scale=rsn[:, t:t + 1]).then_inc(pa_scaled, 1)

            def keep_x1T(t):
                act.wait_ge(x1_tr, t + 1)
                fn(x1T[:, :, t * P:(t + 1) * P],
                   psf[:, (t % 2) * 2048:(t % 2) * 2048 + D].rearrange("p (k n) -> p k n", k=KD),
                   ACT.Copy).then_inc(x1T_ready, 1)

            def keep_query(u):
                act.wait_ge(q_done, u + 1)
                act.wait_ge(score_done, u)
                fn(qs[:, :], ps[:, 6, 0:QD], ACT.Copy).then_inc(qs_ready, 1)

            def gate_exp(u, t):
                act.wait_ge(ids_ready, u + 1)
                fn(expv[:, t, :], best[:, t, :], ACT.Exp, bias=negmax[:, t:t + 1],
                   accum_out=esum[:, t:t + 1]).then_inc(exp_ready, 1)

            def activate(u, t, g):
                i = t % NT
                cols = slice(g * GRP, (g + 1) * GRP)
                act.wait_ge(dots_done, u * TOPK + (g + 1) * GRP)
                if g == 0:
                    act.wait_ge(gates_ready, u + 1)
                fn(gel[:, i, cols], hid[:, i, cols], ACT.Gelu).then_inc(gel_ready, 1)
                act.wait_ge(gel_ready, u * NG + g + 1)
                for c in range(g * GRP, (g + 1) * GRP):
                    fn(actv[:, i, c:c + 1], gel[:, i, c:c + 1], ACT.Copy, scale=gates[:, i, c:c + 1])\
                        .then_inc(actv_ready, 1)
                for c in range(g * GRP, (g + 1) * GRP):
                    act.wait_ge(actv_ready, u * TOPK + c + 1)
                    act.wait_ge(slot_free, u * TOPK + c + 1 + RING - DIAGS)
                    fn(diag[:, c % DIAGS, :], ident[:, :], ACT.Copy, scale=actv[:, i, c:c + 1])\
                        .then_inc(diag_ready, 1)

            def keep_x2T(t):
                act.wait_ge(x2_tr, t + 1)
                fn(x1T[:, :, t * P:(t + 1) * P], psf[:, 2048:3072].rearrange("p (k n) -> p k n", k=KD),
                   ACT.Copy).then_inc(x2T_ready, 1)

            def gate_sigmoid(t, j):
                act.wait_ge(gate_in, 2 * t + j + 1)
                half = x1[:, t, j * HALF:(j + 1) * HALF]
                fn(half, half, ACT.Sigmoid).then_inc(gate_ready, 1)

            scaled_attn(0)
            sqrt_var(1)
            scaled_attn(1)
            keep_x1T(0)
            keep_query(0)
            gate_exp(0, 0)
            scaled_attn(2)
            sqrt_var(1)
            keep_x1T(1)
            keep_query(1)
            scaled_attn(3)
            for t in (2, 3):
                sqrt_var(1)
                keep_x1T(t)

            def unit(h, t, last_head):
                u = h * NT + t
                for g in range(NG):
                    activate(u, t, g)
                    if g == 4 and not (last_head and t == NT - 1):
                        gate_exp(u + 1, (t + 1) % NT)
                    if g == 4 and not (last_head and t + 2 >= NT):
                        keep_query(u + 2)
                    if last_head and t and g == 2:
                        sqrt_var(1)
                    if last_head and t and g == 5:
                        keep_x2T(t - 1)
                if last_head and t:
                    gate_sigmoid(t - 1, 0)
                    gate_sigmoid(t - 1, 1)
                    sqrt_var(1)

            with act.Fori(0, PH - 1) as h:
                for t in range(NT):
                    unit(h, t, False)
            for t in range(NT):
                unit(PH - 1, t, True)
            sqrt_var(1)
            keep_x2T(NT - 1)
            gate_sigmoid(NT - 1, 0)
            gate_sigmoid(NT - 1, 1)
            sqrt_var(1)

        @block.vector
        def _(dve):
            v = nc.vector
            seen = Counter(dve_at)

            def step(ins):
                seen.inc(ins)
                dve.wait_ge(dve_at, seen.base + seen.n)

            def step_to_max(ins):
                seen.inc(ins)
                hold(dve, dve_at, seen.base + seen.n, dve_passed)

            asked = Counter(var_ready)

            def rsqrt(n, out_):
                dve.wait_ge(std_ready, asked.n)
                step(v.reciprocal(rinv[:, 0:n], std[:, 0:n]))
                step(v.tensor_tensor(rtmp[:, 0:n], rinv[:, 0:n], rinv[:, 0:n], ALU.mult))
                step(v.scalar_tensor_tensor(out=rtmp[:, 0:n], in0=rtmp[:, 0:n], scalar=-0.5, in1=var_e[:, 0:n],
                                            op0=ALU.mult, op1=ALU.mult))
                step(v.scalar_tensor_tensor(out=out_, in0=rtmp[:, 0:n], scalar=1.5, in1=rinv[:, 0:n],
                                            op0=ALU.add, op1=ALU.mult))

            def layer_norm_stats(src):
                for j in range(2):
                    step(v.bn_stats(stats[:, j, :], src[:, j * HALF:(j + 1) * HALF]))
                step(v.bn_aggr(aggr[:, 0, :], stats[:, 0:2, :]))
                asked.inc(v.tensor_scalar_add(var_e[:, 0:1], aggr[:, 0, 1:2], EPS))

            def layer_norm_apply(src, g, b, done):
                rsqrt(1, rstd[:, 0:1])
                step(v.tensor_scalar(src, src, aggr[:, 0, 0:1], rstd[:, 0:1], ALU.subtract, ALU.mult))
                step(v.tensor_tensor(src, src, g, ALU.mult))
                v.tensor_tensor(src, src, b, ALU.add).then_inc(done, 1)

            for b in range(WB):
                dve.wait_ge(proj_done, 4 + b + 1)
                v.tensor_copy(kT[:, b, :], ps[:, 4 + b, :]).then_inc(dve_evac, 1)
            for t in range(NT):
                dve.wait_ge(proj_done, 8 + t + 1)
                v.tensor_copy(v_tok[:, t, :], ps[:, t, :]).then_inc(dve_evac, 1)
            for t in range(NT):
                dve.wait_ge(act_evac, 4 + t + 1)
                step(v.bn_stats(stats[:, t, :], gv[:, t, :]))
                step(v.bn_aggr(aggr[:, t, :], stats[:, t, :]))
            asked.inc(v.tensor_scalar_add(var_e[:, 0:NT], aggr[:, :, 1], EPS))
            dve.wait_ge(small_in, 16 * 7)

            def gv_norm(t):
                step(v.tensor_scalar(gv[:, t, :], gv[:, t, :], aggr[:, t, 0:1], rstd[:, t:t + 1],
                                     ALU.subtract, ALU.mult))
                step(v.tensor_tensor(gv[:, t, :], gv[:, t, :], vn_g, ALU.mult))
                i = v.tensor_tensor(gv[:, t, :], gv[:, t, :], vn_b, ALU.add)
                if t == NT - 1:
                    i.then_inc(gvn_ready, 1)

            def take_pair(b):
                dve.wait_ge(attn_sq, b + 1)
                v.tensor_scalar(attnT[:, b, :], ps[:, 6 + b % 2, :], gA[:, b:b + 1], None, ALU.mult)\
                    .then_inc(attn_scaled, 1)

            for h in range(AH):
                z = psf[:, (h % 2) * 1536:(h % 2) * 1536 + ZCOLS]
                dve.wait_ge(log_ready, h + 1)
                v.scalar_tensor_tensor(out=l_buf[:, h % 2, :], in0=z, scalar=0.0, in1=e_buf[:, h % 3, :],
                                       op0=ALU.max, op1=ALU.add).then_inc(l_ready, 1)
                if h == 0:
                    rsqrt(NT, rstd[:, 0:NT])
                if h % 2 == 0:
                    gv_norm(h // 2)
                if h % 2 == 1 and h >= 3:
                    take_pair(h // 2 - 1)
            take_pair(WB - 1)
            for b in range(WB):
                dve.wait_ge(mixed_done, b + 1)
                m = ps[:, b, :].rearrange("p (t n) -> p t n", t=NT)
                bias = bs_b[:, b, :].unsqueeze(1).to_broadcast([P, NT, P])
                dst = l_buf[:, b % 2, 0:S]
                step(v.tensor_tensor(dst.rearrange("p (t n) -> p t n", t=NT), m, bias, ALU.add))
                v.tensor_tensor(guT[:, b, :], dst, guT[:, b, :], ALU.mult).then_inc(gm_ready, 1)
            dve.wait_ge(ssq_done, 1)
            asked.inc(v.tensor_scalar(var_e[:, 0:2 * NT], ps[:, 4, 0:2 * NT], 1.0 / AW, EPS, ALU.mult, ALU.add))
            rsqrt(2 * NT, rsn[:, :])
            v.tensor_copy(rtmp[:, 0:1], rsn[:, 0:1]).then_inc(rms_ready, 1)
            dve.wait_ge(x_in, 16)
            dve.wait_ge(ln1_in, 32)
            def make_x1(t):
                xt = x1[:, t, :]
                dve.wait_ge(pa_scaled, t + 1)
                step(v.scalar_tensor_tensor(out=xt, in0=x_nat[:, t, :], scalar=ALPHA, in1=xt,
                                            op0=ALU.mult, op1=ALU.add))
                dve.wait_ge(pg_done, t + 1)
                step(v.scalar_tensor_tensor(out=xt, in0=psf[:, 2 * 512:2 * 512 + D],
                                            scalar=rsn[:, NT + t:NT + t + 1], in1=xt,
                                            op0=ALU.mult, op1=ALU.add))
                layer_norm_stats(xt)
                layer_norm_apply(xt, ln1_g, ln1_b, x1_ready)

            def rank_keys(u, half):
                if half == 0:
                    hold(dve, score_done, u + 1, dve_passed)
                if True:
                    s = ps[:, 7, half * NKEY:(half + 1) * NKEY]
                    step_to_max(v.max(out=top[:, half, 0:8], in_=s))
                    v.max_index(out=topi[:, half, 0:8], in_max=top[:, half, 0:8], in_values=s)
                    step_to_max(v.match_replace(out=left[:, half, :], in_to_replace=top[:, half, 0:8], in_values=s,
                                         imm_value=NEG))
                    step_to_max(v.max(out=top[:, half, 8:16], in_=left[:, half, :]))
                    k = v.max_index(out=topi[:, half, 8:16], in_max=top[:, half, 8:16], in_values=left[:, half, :])
                    if half == 0:
                        step_to_max(k)
                    else:
                        k.then_inc(score_used, 1)

            def rank_sums(u, t):
                i = t % NT
                first = top[:, 0, :].unsqueeze(2).to_broadcast([P, TOPK, TOPK])
                second = top[:, 1, :].unsqueeze(1).to_broadcast([P, TOPK, TOPK])
                step(v.tensor_tensor(cand[:, :].rearrange("p (x y) -> p x y", x=TOPK), first, second, ALU.add))
                dve.wait_ge(score_used, u + 1)
                step_to_max(v.tensor_copy(topf[:, :, :], topi[:, :, :]))
                step_to_max(v.max(out=best[:, i, 0:8], in_=cand[:, :]))
                v.max_index(out=besti[:, 0:8], in_max=best[:, i, 0:8], in_values=cand[:, :])
                step_to_max(v.match_replace(out=cleft[:, :], in_to_replace=best[:, i, 0:8], in_values=cand[:, :],
                                     imm_value=NEG))
                step_to_max(v.max(out=best[:, i, 8:16], in_=cleft[:, :]))
                step(v.max_index(out=besti[:, 8:16], in_max=best[:, i, 8:16], in_values=cleft[:, :]))

            def rank_ids(u, t):
                i = t % NT
                v.tensor_scalar(negmax[:, i:i + 1], best[:, i, 0:1], -1.0, None, ALU.mult)
                v.tensor_scalar(nib[:, 0, :], besti[:, :], 4, None, ALU.logical_shift_right)
                step(v.tensor_scalar(nib[:, 1, :], besti[:, :], 15, None, ALU.bitwise_and))
                step(v.tensor_copy(nibf[:, :, :], nib[:, :, :]))
                want = nibf[:, :, :].unsqueeze(3).to_broadcast([P, 2, TOPK, TOPK])
                lanes = iota16[:, :].unsqueeze(1).unsqueeze(1).to_broadcast([P, 2, TOPK, TOPK])
                vals = topf[:, :, :].unsqueeze(2).to_broadcast([P, 2, TOPK, TOPK])
                step(v.tensor_tensor(hot[:, :, :, :], lanes, want, ALU.is_equal))
                step(v.tensor_tensor(hot[:, :, :, :], hot[:, :, :, :], vals, ALU.mult))
                step(v.reduce_sum(pick[:, :, :], hot[:, :, :, :], AX.X))
                v.scalar_tensor_tensor(out=ids[:, i, :], in0=pick[:, 0, :], scalar=float(NKEY), in1=pick[:, 1, :],
                                       op0=ALU.mult, op1=ALU.add).then_inc(ids_ready, 1)

            def norm_gates(u, t):
                i = t % NT
                dve.wait_ge(exp_ready, u + 1)
                step(v.reciprocal(erec[:, i:i + 1], esum[:, i:i + 1]))
                v.tensor_scalar(gates[:, i, :], expv[:, i, :], erec[:, i:i + 1], None, ALU.mult)\
                    .then_inc(gates_ready, 1)

            def dots(u, t, g):
                for c in range(g * GRP, (g + 1) * GRP):
                    r = rows[:, c % RING, 0:D]
                    dve.wait_ge(rows_in[c % RING], u * (16 * TOPK // RING) + 16 * (c // RING + 1))
                    v.tensor_tensor_reduce(out=r, in0=r, in1=x1[:, t, :], scale=1.0, scalar=0.0,
                                           op0=ALU.mult, op1=ALU.add,
                                           accum_out=hid[:, t, c:c + 1]).then_inc(dots_done, 1)

            def add_unit(u, t):
                dve.wait_ge(slot_free, u * TOPK + TOPK + RING)
                b = 2 * (t % 2) * 512
                v.tensor_tensor(acc[:, t % NT, :], psf[:, b:b + D], acc[:, t % NT, :], ALU.add)\
                    .then_inc(sum_free, 1)

            def x2_stats(t):
                dve.wait_ge(sum_free, 2 + NT * PH - NT + t + 1)
                if t == 0:
                    dve.wait_ge(tail_in, 16 * 8)
                step(v.scalar_tensor_tensor(out=acc[:, t, :], in0=x1[:, t, :], scalar=ALPHA, in1=acc[:, t, :],
                                            op0=ALU.mult, op1=ALU.add))
                layer_norm_stats(acc[:, t, :])

            def ple_half(t, j):
                half = x1[:, t, j * HALF:(j + 1) * HALF]
                cols = slice(j * HALF, (j + 1) * HALF)
                dve.wait_ge(ple_done, 2 * t + j + 1)
                v.tensor_tensor(half, ps[:, 4, :], b_gate[:, cols], ALU.add).then_inc(gate_in, 1)
                dve.wait_ge(gate_ready, 2 * t + j + 1)
                v.tensor_tensor(half, ps[:, 5, :], half, ALU.mult).then_inc(ple_used, 1)
                dve.wait_ge(ple_used, 2 * t + j + 1)
                step(v.scalar_tensor_tensor(out=acc[:, t, cols], in0=acc[:, t, cols], scalar=ALPHA, in1=half,
                                            op0=ALU.mult, op1=ALU.add))

            def finish(t):
                ple_half(t, 0)
                ple_half(t, 1)
                layer_norm_stats(acc[:, t, :])
                layer_norm_apply(acc[:, t, :], ln3_g, ln3_b, out_ready)

            make_x1(0)
            for half in range(2):
                rank_keys(0, half)
            rank_sums(0, 0)
            rank_ids(0, 0)
            make_x1(1)
            norm_gates(0, 0)
            make_x1(2)
            make_x1(3)
            dve.wait_ge(x1T_ready, NT)
            v.memset(acc, 0.0).then_inc(sum_free, 2)

            def unit(h, t, last_head, first_unit=False):
                u = h * NT + t
                more = not (last_head and t == NT - 1)
                for g in range(NG):
                    dots(u, t, g)
                    if more and g in (0, 1):
                        rank_keys(u + 1, g)
                    if more and g == 2:
                        rank_sums(u + 1, t + 1)
                    if more and g == 3:
                        rank_ids(u + 1, t + 1)
                    if g == 1 and t:
                        add_unit(u - 1, t - 1)
                        if last_head:
                            x2_stats(t - 1)
                    if g == 2 and last_head and t:
                        layer_norm_apply(acc[:, t - 1, :], ln2_g, ln2_b, x2_ready)
                    if more and g == 5:
                        norm_gates(u + 1, t + 1)
                if last_head and t:
                    finish(t - 1)
                if t == NT - 1:
                    add_unit(u, t)

            before = seen.n
            with dve.Fori(0, PH - 1) as h:
                seen.base, seen.n = h * HEAD_STEPS + before, 0
                for t in range(NT):
                    unit(h, t, False)
                assert seen.n == HEAD_STEPS
            seen.base, seen.n = 0, before + HEAD_STEPS * (PH - 1)
            for t in range(NT):
                unit(PH - 1, t, True)
            x2_stats(NT - 1)
            layer_norm_apply(acc[:, NT - 1, :], ln2_g, ln2_b, x2_ready)
            finish(NT - 1)


def kernel(**inputs):
    import concourse.bacc as _bacc
    from concourse.bass_utils import run_bass_kernel_spmd as _run

    f = {k: np.asarray(x) for k, x in inputs.items()}

    def chunks(w):
        return w.reshape(-1, P, w.shape[-1]).transpose(1, 0, 2)

    def blocks(w):
        return w.reshape(KD, P, WB, P).transpose(1, 2, 0, 3).reshape(P, -1)

    w = f["w_in"][0]
    x = f["x"][0]
    arrays = {
        "xT": chunks(x.T),
        "x": x.reshape(NT, P, D).transpose(1, 0, 2),
        "w_q": blocks(w[:, 0:AW]),
        "w_k": blocks(w[:, AW:2 * AW]),
        "w_v": chunks(w[:, 2 * AW:3 * AW]).reshape(P, -1),
        "w_gu": blocks(w[:, 3 * AW:4 * AW]),
        "w_gv": chunks(w[:, 4 * AW:5 * AW]).reshape(P, -1),
        "wsT": f["gmlp_ws"][0].transpose(2, 0, 1),
        "gA": f["attn_out_g"][0].reshape(WB, P).T,
        "gG": f["gmlp_out_g"][0].reshape(WB, P).T,
        "w_out": chunks(f["w_out"][0]),
        "wq": f["peer_wq"][0].reshape(KD, P, PH, QD).transpose(2, 1, 0, 3),
        "subk": f["peer_subkeys"][0].transpose(3, 0, 1, 2).reshape(P, -1),
        "uv": np.concatenate([f["peer_u"][0], f["peer_v"][0]], axis=1),
        "w_gate": chunks(f["ple_wgate"][0]),
        "w_proj": chunks(f["ple_wproj"][0]),
        "pT": chunks(f["p"][0, 0].T),
    }
    for name in ("gmlp_vn_g", "gmlp_vn_b", "gmlp_bs", "ln1_g", "ln1_b", "ln2_g", "ln2_b", "ln3_g", "ln3_b",
                 "ple_bgate"):
        arrays[name] = f[name]
    nc = _bacc.Bacc("TRN2", target_bir_lowering=False, num_devices=1)
    data, aps = {}, {}
    for name, array in arrays.items():
        data[f"in_{name}"] = np.ascontiguousarray(array)
        aps[name] = nc.dram_tensor(f"in_{name}", array.shape, FP32, kind="ExternalInput").ap()
    out = nc.dram_tensor("out_0", (1, S, D), FP32, kind="ExternalOutput").ap()
    build(nc, aps, out)
    return _run(nc, [data], core_ids=[0]).results[0]["out_0"]
```

```python
import math
from contextlib import ExitStack

import numpy as np
import concourse.bass as bass
from concourse import mybir

FP32 = mybir.dt.float32
U32 = mybir.dt.uint32
I32 = mybir.dt.int32
ALU = mybir.AluOpType
ACT = mybir.ActivationFunctionType
AX = mybir.AxisListType

P = 128
D = 1024
S = 512
NT = S // P
KD = D // P
AH, DH = 8, 64
AW = AH * DH
G = 8
WB = AW // P
PH, TOPK, NKEY = 8, 16, 128
QD = 256
PLE = 256
EPS = 1e-5
ALPHA = 2.0 ** 0.25
QSCALE = 1.0 / math.sqrt(DH)
NEG = -3.0e38
ARENA = 37632

RING = 8
GRP = 2
NG = TOPK // GRP
RANK_STEPS = 18
HEAD_STEPS = NT * (RANK_STEPS + 1)
DIAGS = 4
HALF = D // 2

ZOFF = {0: 0, 1: 512, 3: 896, 2: 1024}
ZCOLS = 1280


def pa_bank(t):
    return 0 if t == 0 else 4


def pg_bank(t):
    return 2 if t < 2 else 4


def x2_bank(t):
    return 4 if t < NT - 1 else 6


def gate_bank(t):
    return 4 if t < NT - 1 else 2


def embedding_bank(t):
    return 4 if t < NT - 1 else 0


def zlen(s):
    return S - P * s


class Counter:

    def __init__(self, sem):
        self.sem, self.n, self.base = sem, 0, 0

    def inc(self, instruction, by=1):
        instruction.then_inc(self.sem, by)
        self.n += by


def hold(eng, sem, value, passed):
    eng.wait_ge(sem, value)
    eng.sem_inc(passed, 1)


def build(nc, a, out):
    ctx = ExitStack()
    with ctx:
        def sb(name, shape, dt=FP32):
            return ctx.enter_context(nc.sbuf_tensor(name, shape, dt))

        def sem(name):
            return ctx.enter_context(nc.semaphore(name))

        x1 = sb("x1", [P, NT, D])
        x1T = sb("x1T", [P, KD, S])
        wq_head = sb("wq_head", [P, KD, QD])
        subk = sb("subk", [P, PH * 2 * NKEY])
        ident = sb("ident", [P, P])
        neg_tri = sb("neg_tri", [P, P])
        neg_one = sb("neg_one", [P, P])
        ones = sb("ones", [P, 1])
        iota16 = sb("iota16", [P, TOPK])
        gA = sb("gA", [P, WB])
        gG = sb("gG", [P, WB])
        stats = sb("stats", [P, 4, 6])
        aggr = sb("aggr", [P, NT + 1, 2])
        var_e = sb("var_e", [P, 8])
        std = sb("std", [P, 8])
        rinv = sb("rinv", [P, 8])
        rtmp = sb("rtmp", [P, 8])
        rstd = sb("rstd", [P, 8])
        rsn = sb("rsn", [P, 2 * NT])

        arena = sb("arena", [P, ARENA])
        at = [0]

        def take(n):
            at[0] += n
            return arena[:, at[0] - n:at[0]]

        ring_w = take(8192)
        wgrp = [ring_w[:, 0:4096], ring_w[:, 4096:8192]]
        w_out = ring_w.rearrange("p (c n) -> p c n", c=8)
        ln1_g, ln1_b = take(D), take(D)
        qk_flat = take(4096)
        qT = qk_flat[:, 0:2048].rearrange("p (b s) -> p b s", b=WB)
        kT = qk_flat[:, 2048:4096].rearrange("p (b s) -> p b s", b=WB)
        x_nat = qk_flat.rearrange("p (t d) -> p t d", t=NT)
        attnT = take(2048).rearrange("p (b s) -> p b s", b=WB)
        gmT = take(2048).rearrange("p (b s) -> p b s", b=WB)
        live = at[0]
        xT_flat = take(4096)
        xT = xT_flat.rearrange("p (k s) -> p k s", k=KD)
        squares = xT_flat.rearrange("p (c s) -> p c s", c=8)
        guT = take(2048).rearrange("p (b s) -> p b s", b=WB)
        v_tok = take(2048).rearrange("p (t c) -> p t c", t=NT)
        gv = take(2048).rearrange("p (t c) -> p t c", t=NT)
        wsT = take(1024).rearrange("p (g t) -> p g t", g=G)
        vn_g, vn_b = take(AW), take(AW)
        bs_b = take(AW).rearrange("p (b t) -> p b t", b=WB)
        e_buf = take(3 * ZCOLS).rearrange("p (i n) -> p i n", i=3)
        l_buf = take(2 * ZCOLS).rearrange("p (i n) -> p i n", i=2)
        dead = at[0]

        at[0] = live
        rows = take(RING * 2 * D).rearrange("p (r n) -> p r n", r=RING)
        assert at[0] <= dead
        pT = take(2 * S).rearrange("p (k s) -> p k s", k=2)
        b_gate = take(D)
        assert at[0] <= ARENA
        acc = x_nat
        at[0] = 0
        w_gate = take(KD * D).rearrange("p (k n) -> p k n", k=KD)
        ln2_g, ln2_b = take(D), take(D)
        take(NT * D)
        w_proj = take(2 * D).rearrange("p (k n) -> p k n", k=2)
        ln3_g, ln3_b = take(D), take(D)
        assert at[0] <= live

        gains = (ln2_g, ln2_b, b_gate, ln3_g, ln3_b)

        qs = sb("qs", [P, QD])
        left = sb("left", [P, 2, NKEY])
        top = sb("top", [P, 2, TOPK])
        topi = sb("topi", [P, 2, TOPK], U32)
        topf = sb("topf", [P, 2, TOPK])
        cand = sb("cand", [P, TOPK * TOPK])
        cleft = sb("cleft", [P, TOPK * TOPK])
        best = sb("best", [P, NT, TOPK])
        besti = sb("besti", [P, TOPK], U32)
        nib = sb("nib", [P, 2, TOPK], U32)
        nibf = sb("nibf", [P, 2, TOPK])
        hot = sb("hot", [P, 2, TOPK, TOPK])
        pick = sb("pick", [P, 2, TOPK])
        ids = sb("ids", [P, NT, TOPK], I32)
        negmax = sb("negmax", [P, NT])
        expv = sb("expv", [P, NT, TOPK])
        esum = sb("esum", [P, NT])
        erec = sb("erec", [P, NT])
        gates = sb("gates", [P, NT, TOPK])
        hid = sb("hid", [P, NT, TOPK])
        gel = sb("gel", [P, NT, TOPK])
        actv = sb("actv", [P, NT, TOPK])
        diag = sb("diag", [P, DIAGS, P])

        ps = ctx.enter_context(nc.psum_tensor("ps", [P, 8, 512], FP32))
        psf = ps[:, :, :].rearrange("p b n -> p (b n)")

        xT_in = [sem(f"xT_in{i}") for i in range(4)]
        w_in = [sem(f"w_in{i}") for i in range(8)]
        small_in = sem("small_in")
        wout_in = [sem("wout_in0"), sem("wout_in1")]
        x_in = sem("x_in")
        ln1_in = sem("ln1_in")
        subk_in = sem("subk_in")
        wq_in = sem("wq_in")
        tail_in = sem("tail_in")
        const_ready = sem("const_ready")
        ws_masked = sem("ws_masked")
        proj_done = sem("proj_done")
        act_evac = sem("act_evac")
        dve_evac = sem("dve_evac")
        z_done = sem("z_done")
        log_ready = sem("log_ready")
        l_ready = sem("l_ready")
        l_masked = sem("l_masked")
        arg_done = sem("arg_done")
        a_ready = sem("a_ready")
        a_masked = sem("a_masked")
        av_done = sem("av_done")
        attn_sq = sem("attn_sq")
        attn_scaled = sem("attn_scaled")
        gvn_ready = sem("gvn_ready")
        mixed_done = sem("mixed_done")
        gm_ready = sem("gm_ready")
        gm_out = sem("gm_out")
        gm_sq = sem("gm_sq")
        sq_added = sem("sq_added")
        ssq_done = sem("ssq_done")
        rms_ready = sem("rms_ready")
        pa_done = sem("pa_done")
        pg_done = sem("pg_done")
        pa_scaled = sem("pa_scaled")
        x1_ready = sem("x1_ready")
        x1_tr = sem("x1_tr")
        x1T_ready = sem("x1T_ready")
        var_ready = sem("var_ready")
        std_ready = sem("std_ready")
        dve_at = sem("dve_at")
        act_at = sem("act_at")

        q_done = sem("q_done")
        qs_ready = sem("qs_ready")
        score_done = sem("score_done")
        score_used = sem("score_used")
        ids_ready = sem("ids_ready")
        exp_ready = sem("exp_ready")
        gates_ready = sem("gates_ready")
        rows_in = [sem(f"rows_in{i}") for i in range(RING)]
        dots_done = sem("dots_done")
        gel_ready = sem("gel_ready")
        actv_ready = sem("actv_ready")
        diag_ready = sem("diag_ready")
        slot_free = sem("slot_free")
        sum_free = sem("sum_free")
        x2_ready = sem("x2_ready")
        x2_tr = sem("x2_tr")
        x2T_ready = sem("x2T_ready")
        gain_in = sem("gain_in")
        gain_spread = sem("gain_spread")
        gain_kept = sem("gain_kept")
        gate_done = sem("gate_done")
        embedding_done = sem("embedding_done")
        gate_in = sem("gate_in")
        gate_ready = sem("gate_ready")
        ple_used = sem("ple_used")
        out_ready = sem("out_ready")
        out_done = sem("out_done")
        dve_passed = sem("dve_passed")
        pool_passed = sem("pool_passed")

        block = ctx.enter_context(nc.Block())

        @block.sync
        def _(sp):
            sp.dma_start(wgrp[0][:, 0:D], a["w_q"][:, 0:D]).then_inc(w_in[0], 16)
            for i in range(4):
                sp.dma_start(xT[:, 2 * i:2 * i + 2, :], a["xT"][:, 2 * i:2 * i + 2, :]).then_inc(xT_in[i], 16)
            for b in range(1, WB):
                sp.dma_start(wgrp[0][:, b * D:(b + 1) * D],
                             a["w_q"][:, b * D:(b + 1) * D]).then_inc(w_in[b], 16)
            sp.dma_start(wgrp[1], a["w_k"][:, :]).then_inc(w_in[4], 16)
            sp.dma_start(wsT, a["wsT"][:, :, :]).then_inc(small_in, 16)
            sp.dma_start(vn_g, a["gmlp_vn_g"][0, :].partition_broadcast(P)).then_inc(small_in, 16)
            sp.dma_start(vn_b, a["gmlp_vn_b"][0, :].partition_broadcast(P)).then_inc(small_in, 16)
            for half in range(2):
                sp.dma_start(bs_b[half * DH:(half + 1) * DH, :, :],
                             a["gmlp_bs"][0].rearrange("(b h) t -> h b t", h=2)[half]
                             .partition_broadcast(DH)).then_inc(small_in, 16)
            sp.dma_start(gA[:, :], a["gA"][:, :]).then_inc(small_in, 16)
            sp.dma_start(gG[:, :], a["gG"][:, :]).then_inc(small_in, 16)
            sp.dma_start(subk[:, :], a["subk"][:, :]).then_inc(subk_in, 16)
            sp.dma_start(wq_head[:, :, :], a["wq"][0]).then_inc(wq_in, 16)
            sp.wait_ge(proj_done, 4)
            sp.dma_start(wgrp[0], a["w_v"][:, :]).then_inc(w_in[5], 16)
            sp.wait_ge(proj_done, 8)
            sp.dma_start(wgrp[1], a["w_gv"][:, :]).then_inc(w_in[6], 16)
            sp.wait_ge(proj_done, 12)
            sp.dma_start(wgrp[0], a["w_gu"][:, :]).then_inc(w_in[7], 16)
            sp.dma_start(ln1_g, a["ln1_g"][0, :].partition_broadcast(P)).then_inc(ln1_in, 16)
            sp.dma_start(ln1_b, a["ln1_b"][0, :].partition_broadcast(P)).then_inc(ln1_in, 16)
            sp.wait_ge(proj_done, 16)
            sp.dma_start(w_out[:, 4:8, :], a["w_out"][:, 4:8, :]).then_inc(wout_in[1], 16)
            sp.wait_ge(proj_done, 20)
            sp.dma_start(w_out[:, 0:4, :], a["w_out"][:, 0:4, :]).then_inc(wout_in[0], 16)
            sp.wait_ge(arg_done, AH)
            sp.dma_start(x_nat, a["x"][:, :, :]).then_inc(x_in, 16)
            sp.wait_ge(x1T_ready, 2 * NT)
            for dst, name in zip(gains, ("ln2_g", "ln2_b", "ple_bgate", "ln3_g", "ln3_b")):
                sp.dma_start(dst[0:1, :], a[name][:, :]).then_inc(gain_in, 16)
            for dst, src in ((w_gate, a["w_gate"][:, :, :]), (w_proj, a["w_proj"][:, :, :]), (pT, a["pT"][:, :, :])):
                sp.dma_start(dst, src).then_inc(tail_in, 16)
            with sp.Fori(0, PH - 1) as h:
                sp.wait_ge(q_done, h * NT + NT)
                sp.dma_start(wq_head[:, :, :], a["wq"][bass.ds(h + 1, 1)].rearrange("h p k n -> (h p) k n"))\
                  .then_inc(wq_in, 16)
            for t in range(NT):
                for j in range(2):
                    sp.wait_ge(out_ready, 2 * t + j + 1)
                    sp.dma_start(out[0, t * P:(t + 1) * P, j * HALF:(j + 1) * HALF],
                                 acc[:, t, j * HALF:(j + 1) * HALF]).then_inc(out_done, 16)
            sp.wait_ge(out_done, 2 * 16 * NT)

        @block.gpsimd
        def _(pool):
            nc.gpsimd.memset(ident[:, :], 0.0).then_inc(const_ready, 1)
            nc.gpsimd.memset(neg_tri[:, :], -1.0).then_inc(const_ready, 1)
            nc.gpsimd.memset(neg_one[:, :], -1.0).then_inc(const_ready, 1)
            nc.gpsimd.memset(ones[:, :], 1.0).then_inc(const_ready, 1)
            nc.gpsimd.iota(iota16[:, :], pattern=[[1, TOPK]], base=0, channel_multiplier=0,
                           allow_small_or_imprecise_dtypes=True).then_inc(const_ready, 1)
            pool.wait_ge(const_ready, 5)
            nc.gpsimd.affine_select(out=ident[:, :], in_=ident[:, :], compare_op=ALU.not_equal, fill=1.0,
                                    base=0, pattern=[[-1, P]], channel_multiplier=1).then_inc(const_ready, 1)
            nc.gpsimd.affine_select(out=neg_tri[:, :], in_=neg_tri[:, :], compare_op=ALU.is_ge, fill=0.0,
                                    base=0, pattern=[[-1, P]], channel_multiplier=1).then_inc(const_ready, 1)
            pool.wait_ge(small_in, 16 * 7)
            nc.gpsimd.affine_select(out=wsT, in_=wsT, compare_op=ALU.is_ge, fill=0.0, base=0,
                                    pattern=[[0, G], [1, P]], channel_multiplier=-1).then_inc(ws_masked, 1)

            def keep_past(buf, s, done):
                blk = buf[:, ZOFF[s]:ZOFF[s] + P]
                nc.gpsimd.affine_select(out=blk, in_=blk, compare_op=ALU.is_gt, fill=0.0, base=0,
                                        pattern=[[1, P]], channel_multiplier=-1).then_inc(done, 1)

            for h in range(AH + 1):
                if h < AH:
                    pool.wait_ge(l_ready, h + 1)
                    for s in range(NT):
                        keep_past(l_buf[:, h % 2, :], s, l_masked)
                if h >= 1:
                    pool.wait_ge(a_ready, h)
                    for s in range(NT):
                        keep_past(e_buf[:, (h - 1) % 3, :], s, a_masked)

            def gather_unit(u, t):
                pool.wait_ge(ids_ready, u + 1)
                for c in range(TOPK):
                    hold(pool, slot_free, u * TOPK + c + 1, pool_passed)
                    nc.gpsimd.indirect_dma_start(
                        out=rows[:, c % RING, :], out_offset=None, in_=a["uv"][:, :],
                        in_offset=bass.IndirectOffsetOnAxis(ap=ids[:, t, c:c + 1], axis=0),
                    ).then_inc(rows_in[c % RING], 16)

            with pool.Fori(0, PH) as h:
                for t in range(NT):
                    gather_unit(h * NT + t, t)

        @block.tensor
        def _(pe):
            mm = nc.tensor.matmul

            def project_T(bank, w, j, first=False):
                for k in range(KD):
                    if first and k % 2 == 0:
                        pe.wait_ge(xT_in[k // 2], 16)
                    i = mm(ps[:, bank, :], w[:, j * D + k * P:j * D + (k + 1) * P], xT[:, k, :],
                           start=(k == 0), stop=(k == KD - 1))
                i.then_inc(proj_done, 1)

            def project_tok(bank, w, t):
                for k in range(KD):
                    i = mm(ps[:, bank, :], xT[:, k, t * P:(t + 1) * P], w[:, k * AW:(k + 1) * AW],
                           start=(k == 0), stop=(k == KD - 1))
                i.then_inc(proj_done, 1)

            for b in range(WB):
                pe.wait_ge(w_in[b], 16)
                project_T(b, wgrp[0], b, first=(b == 0))
            pe.wait_ge(w_in[4], 16)
            for b in range(WB):
                project_T(4 + b, wgrp[1], b)
            pe.wait_ge(w_in[5], 16)
            for t in range(NT):
                pe.wait_ge(act_evac, t + 1)
                project_tok(t, wgrp[0], t)
            pe.wait_ge(w_in[6], 16)
            for t in range(NT):
                pe.wait_ge(dve_evac, t + 1)
                project_tok(4 + t, wgrp[1], t)

            def z_cols(h, s, n0=0):
                base = (h % 2) * 3 * 512 + ZOFF[s]
                return psf[:, base + n0:base + zlen(s)]

            def scores(h, s, start):
                r = slice(DH * (h % 2), DH * (h % 2) + DH)
                return mm(z_cols(h, s), kT[r, h // 2, s * P:(s + 1) * P], qT[r, h // 2, s * P:S],
                          start=start, stop=False, skip_group_check=True)

            def open_scores(h):
                if h >= 2:
                    pe.wait_ge(a_ready, h - 1)
                for s in (0, 1, 3, 2):
                    i = scores(h, s, s != 3)
                i.then_inc(z_done, 1)

            def subtract_sums(h):
                pe.wait_ge(l_masked, NT * (h + 1))
                for s in (0, 1, 3, 2):
                    for j in range(s, NT):
                        n0 = (j - s) * P
                        i = mm(z_cols(h, s, n0), (neg_tri if j == s else neg_one)[:, :],
                               l_buf[:, h % 2, ZOFF[j]:ZOFF[j] + zlen(j)], start=False,
                               stop=(j == NT - 1), skip_group_check=True)
                i.then_inc(arg_done, 1)

            def weigh_values(h):
                pe.wait_ge(a_masked, NT * (h + 1))
                if h >= 4 and h % 2 == 0:
                    pe.wait_ge(attn_sq, h // 2 - 1)
                    pe.wait_ge(attn_scaled, h // 2 - 1)
                r = slice(DH * (h % 2), DH * (h % 2) + DH)
                for s in range(NT):
                    i = mm(ps[r, 6 + (h // 2) % 2, s * P:S], v_tok[:, s, h * DH:(h + 1) * DH],
                           e_buf[:, h % 3, ZOFF[s]:ZOFF[s] + zlen(s)], start=(s == 0), stop=(s == NT - 1),
                           skip_group_check=True)
                i.then_inc(av_done, 1)

            pe.wait_ge(const_ready, 7)
            pe.wait_ge(dve_evac, 7)
            open_scores(0)
            pe.wait_ge(w_in[7], 16)
            pe.wait_ge(dve_evac, 8)
            project_T(3, wgrp[0], 0)
            for b in range(1, WB):
                pe.wait_ge(act_evac, 4 + b)
                project_T(3 + b, wgrp[0], b)
            pe.wait_ge(act_evac, 4 + NT + WB)
            for h in range(AH + 1):
                if h + 1 < AH:
                    open_scores(h + 1)
                if h < AH:
                    subtract_sums(h)
                if h >= 1:
                    weigh_values(h - 1)

            pe.wait_ge(ws_masked, 1)
            pe.wait_ge(gvn_ready, 1)
            for b in range(WB):
                for g in (2 * b, 2 * b + 1):
                    r = slice(DH * (g % 2), DH * (g % 2) + DH)
                    for t in range(NT):
                        i = mm(ps[r, b, t * P:(t + 1) * P], gv[:, t, g * DH:(g + 1) * DH], wsT[:, g, :],
                               start=(t == 0), stop=True, skip_group_check=True)
                i.then_inc(mixed_done, 1)

            def sum_squares(kind):
                pe.wait_ge(sq_added, (kind + 1) * (WB - 1))
                for t in range(NT):
                    i = mm(ps[:, 4, kind * NT + t:kind * NT + t + 1],
                           squares[:, kind * WB, t * P:(t + 1) * P], ones[:, :], start=True, stop=True)
                if kind == 1:
                    i.then_inc(ssq_done, 1)

            def project_half(kind, t, j):
                src = (attnT, gmT)[kind]
                first_bank = (pa_bank(t), pg_bank(t))[kind]
                for c in range(WB):
                    i = mm(ps[:, first_bank + j, :], src[:, c, t * P:(t + 1) * P],
                           w_out[:, kind * WB + c, j * HALF:(j + 1) * HALF],
                           start=(c == 0), stop=(c == WB - 1))
                if j == 1:
                    i.then_inc((pa_done, pg_done)[kind], 1)

            def project_out(kind, t):
                project_half(kind, t, 0)
                project_half(kind, t, 1)

            def transpose_x1(t):
                for j in range(2):
                    pe.wait_ge(x1_ready, 2 * t + j + 1)
                    for k in range(4 * j, 4 * j + 4):
                        i = nc.tensor.transpose(ps[:, pa_bank(t) + j, (k % 4) * P:(k % 4 + 1) * P],
                                                x1[:, t, k * P:(k + 1) * P], ident[:, :])
                    i.then_inc(x1_tr, 1)

            def query(h, t, u):
                if t == 0:
                    pe.wait_ge(wq_in, h * 16 + 16)
                pe.wait_ge(qs_ready, u)
                for half in range(2):
                    for k in range(KD):
                        i = mm(ps[:, 6, half * P:(half + 1) * P], wq_head[:, k, half * P:(half + 1) * P],
                               x1T[:, k, t * P:(t + 1) * P], start=(k == 0), stop=(k == KD - 1))
                i.then_inc(q_done, 1)

            def key_scores(h, t, u):
                pe.wait_ge(qs_ready, u + 1)
                pe.wait_ge(score_used, u)
                for half in range(2):
                    i = mm(ps[:, 7, half * P:(half + 1) * P], qs[:, half * P:(half + 1) * P],
                           subk[:, bass.ds((h * 2 + half) * NKEY, NKEY)], start=True, stop=True)
                i.then_inc(score_done, 1)

            def spread_gain(i):
                if i == 0:
                    pe.wait_ge(gain_in, 16 * len(gains))
                pe.wait_ge(gain_kept, i)
                for j in range(2):
                    k = mm(ps[:, 4 + j, :], neg_one[0:1, :], gains[i][0:1, j * HALF:(j + 1) * HALF],
                           start=True, stop=True)
                k.then_inc(gain_spread, 1)

            def combine(u, t, c):
                if c == 0:
                    pe.wait_ge(sum_free, u + 1)
                pe.wait_ge(diag_ready, u * TOPK + c + 1)
                for j in range(2):
                    i = mm(ps[:, 2 * (t % 2) + j, :], diag[:, c % DIAGS, :],
                           rows[:, c % RING, D + j * HALF:D + (j + 1) * HALF],
                           start=(c == 0), stop=(c == TOPK - 1))
                i.then_inc(slot_free, 1)

            def x2_transposes(t):
                if 0 < t < NT - 1:
                    pe.wait_ge(ple_used, 2 * t)
                for j in range(2):
                    pe.wait_ge(x2_ready, 2 * t + j + 1)
                    for k in range(4 * j, 4 * j + 4):
                        i = nc.tensor.transpose(ps[:, x2_bank(t) + j, (k % 4) * P:(k % 4 + 1) * P],
                                                acc[:, t, k * P:(k + 1) * P], ident[:, :])
                    i.then_inc(x2_tr, 1)

            def embedding_products(t):
                for j in range(2):
                    if t < NT - 1:
                        pe.wait_ge(gate_in, 2 * t + j + 1)
                    for k in range(2):
                        i = mm(ps[:, embedding_bank(t) + j, :], pT[:, k, t * P:(t + 1) * P],
                               w_proj[:, k, j * HALF:(j + 1) * HALF], start=(k == 0), stop=(k == 1))
                    i.then_inc(embedding_done, 1)

            def gate_product(t, j, k0, k1):
                for k in range(k0, k1):
                    i = mm(ps[:, gate_bank(t) + j, :], x1T[:, k, t * P:(t + 1) * P],
                           w_gate[:, k, j * HALF:(j + 1) * HALF], start=(k == 0), stop=(k == KD - 1),
                           skip_group_check=True)
                if k1 == KD:
                    i.then_inc(gate_done, 1)

            pe.wait_ge(wout_in[0], 16)
            pe.wait_ge(wout_in[1], 16)
            pe.wait_ge(attn_scaled, WB)
            pe.wait_ge(gm_ready, 2)
            project_out(0, 0)
            pe.wait_ge(gm_out, WB)
            pe.wait_ge(gm_ready, WB)
            project_half(1, 0, 0)
            sum_squares(0)
            sum_squares(1)
            project_half(1, 0, 1)
            nc.tensor.matmul(ps[:, 5, 0:1], ident[:, :], ones[:, :], start=True, stop=True)\
              .then_inc(slot_free, RING)
            pe.wait_ge(rms_ready, 1)
            project_out(0, 1)
            pe.wait_ge(subk_in, 16)
            for t in range(2):
                transpose_x1(t)
                pe.wait_ge(x1T_ready, 2 * t + 2)
                query(0, t, t)
                key_scores(0, t, t)
                if t == 0:
                    project_out(1, 1)

            def unit(h, t, last_head, first_head=False):
                u = h * NT + t
                ahead = (h, t + 2, u + 2) if t + 2 < NT else (h + 1, t + 2 - NT, u + 2)
                more = not (last_head and t + 2 >= NT)
                for c in range(TOPK):
                    combine(u, t, c)
                    if first_head and t < 2:
                        if c in (0, 1):
                            project_half(0, t + 2, c)
                        if c == 3:
                            pe.wait_ge(pa_scaled, t + 3)
                        if c in (3, 4):
                            project_half(1, t + 2, c - 3)
                        if c == 11:
                            transpose_x1(t + 2)
                        if c == 13:
                            pe.wait_ge(x1T_ready, 2 * t + 6)
                            query(*ahead)
                        if c == 15:
                            key_scores(*ahead)
                    else:
                        if c == (2 if last_head else 9) and more:
                            query(*ahead)
                        if c == (5 if last_head else 12) and more:
                            key_scores(*ahead)
                    if first_head and t == NT - 1 and c % 2 and 3 <= c < 3 + 2 * len(gains):
                        spread_gain((c - 3) // 2)
                    if last_head and t:
                        if c == 5:
                            x2_transposes(t - 1)
                        if c == 7:
                            pe.wait_ge(x2T_ready, 2 * t)
                            if t == 1:
                                pe.wait_ge(tail_in, 16 * 3)
                        if 7 <= c < 11:
                            gate_product(t - 1, (c - 7) // 2, (c - 7) % 2 * 4, (c - 7) % 2 * 4 + 4)
                        if c == 14 and t < NT - 1:
                            embedding_products(t - 1)

            for t in range(NT):
                unit(0, t, False, True)
            with pe.Fori(1, PH - 1) as h:
                for t in range(NT):
                    unit(h, t, False)
            for t in range(NT):
                unit(PH - 1, t, True)
            embedding_products(NT - 2)
            pe.wait_ge(sum_free, 1 + NT * PH)
            embedding_products(NT - 1)
            pe.wait_ge(qs_ready, NT * PH)
            pe.wait_ge(score_used, NT * PH)
            x2_transposes(NT - 1)
            pe.wait_ge(sum_free, 2 + NT * PH)
            for j in range(2):
                pe.wait_ge(x2T_ready, 2 * NT - 1 + j)
                gate_product(NT - 1, 0, 4 * j, 4 * j + 4)
            gate_product(NT - 1, 1, 0, KD)

        @block.scalar
        def _(act):
            fn = nc.scalar.activation
            for b in range(WB):
                act.wait_ge(proj_done, b + 1)
                fn(qT[:, b, :], ps[:, b, :], ACT.Copy, scale=QSCALE).then_inc(act_evac, 1)
            for t in range(NT):
                act.wait_ge(proj_done, 12 + t + 1)
                fn(gv[:, t, :], ps[:, 4 + t, :], ACT.Gelu).then_inc(act_evac, 1)
            stds = Counter(std_ready)

            def sqrt_var(n):
                act.wait_ge(var_ready, stds.n + 1)
                stds.inc(fn(std[:, 0:n], var_e[:, 0:n], ACT.Sqrt))

            def log_terms(h):
                e = e_buf[:, h % 3, :]
                act.wait_ge(z_done, h + 1)
                if h >= 3:
                    act.wait_ge(av_done, h - 2)
                fn(e, psf[:, (h % 2) * 1536:(h % 2) * 1536 + ZCOLS], ACT.Abs).then_inc(act_at, 1)
                act.wait_ge(act_at, 2 * h + 1)
                fn(e, e, ACT.Exp, scale=-1.0).then_inc(act_at, 1)
                act.wait_ge(act_at, 2 * h + 2)
                fn(e, e, ACT.Ln, bias=1.0).then_inc(log_ready, 1)

            act.preload_act_table_set("natural_log_exp_and_others")
            log_terms(0)
            for b in range(WB):
                act.wait_ge(proj_done, 16 + b + 1)
                fn(guT[:, b, :], ps[:, 3 + b, :], ACT.Gelu).then_inc(act_evac, 1)
            sqrt_var(NT)
            act.preload_act_table_set("natural_log_exp_and_others")
            for h in range(1, AH + 1):
                if h < AH:
                    log_terms(h)
                g = h - 1
                act.wait_ge(arg_done, g + 1)
                fn(e_buf[:, g % 3, :], psf[:, (g % 2) * 1536:(g % 2) * 1536 + ZCOLS], ACT.Exp)\
                    .then_inc(a_ready, 1)
                if g % 2 == 0 and g >= 2:
                    b = g // 2 - 1
                    act.wait_ge(av_done, g)
                    fn(squares[:, b, :], ps[:, 6 + b % 2, :], ACT.Square).then_inc(attn_sq, 1)
            act.wait_ge(av_done, AH)
            fn(squares[:, WB - 1, :], ps[:, 6 + (WB - 1) % 2, :], ACT.Square).then_inc(attn_sq, 1)
            for b in range(WB):
                act.wait_ge(gm_ready, b + 1)
                fn(squares[:, WB + b, :], guT[:, b, :], ACT.Square).then_inc(gm_sq, 1)
                fn(gmT[:, b, :], guT[:, b, :], ACT.Copy, scale=gG[:, b:b + 1]).then_inc(gm_out, 1)
            sqrt_var(2 * NT)

            def scaled_attn(t):
                act.wait_ge(pa_done, t + 1)
                act.wait_ge(rms_ready, 1)
                fn(x1[:, t, :], psf[:, pa_bank(t) * 512:pa_bank(t) * 512 + D], ACT.Copy,
                   scale=rsn[:, t:t + 1]).then_inc(pa_scaled, 1)

            def keep_x1T(t):
                for j in range(2):
                    act.wait_ge(x1_tr, 2 * t + j + 1)
                    fn(x1T[:, 4 * j:4 * j + 4, t * P:(t + 1) * P],
                       ps[:, pa_bank(t) + j, :].rearrange("p (k n) -> p k n", k=4), ACT.Copy)\
                        .then_inc(x1T_ready, 1)

            def keep_query(u):
                act.wait_ge(q_done, u + 1)
                act.wait_ge(score_done, u)
                fn(qs[:, :], ps[:, 6, 0:QD], ACT.Copy).then_inc(qs_ready, 1)

            def gate_exp(u, t):
                act.wait_ge(ids_ready, u + 1)
                fn(expv[:, t, :], best[:, t, :], ACT.Exp, bias=negmax[:, t:t + 1],
                   accum_out=esum[:, t:t + 1]).then_inc(exp_ready, 1)

            def keep_gain(i):
                act.wait_ge(gain_spread, i + 1)
                fn(gains[i], psf[:, 4 * 512:4 * 512 + D], ACT.Copy, scale=-1.0).then_inc(gain_kept, 1)

            def activate(u, t, g):
                i = t % NT
                cols = slice(g * GRP, (g + 1) * GRP)
                act.wait_ge(dots_done, u * TOPK + (g + 1) * GRP)
                if g == 0:
                    act.wait_ge(gates_ready, u + 1)
                fn(gel[:, i, cols], hid[:, i, cols], ACT.Gelu).then_inc(gel_ready, 1)
                act.wait_ge(gel_ready, u * NG + g + 1)
                for c in range(g * GRP, (g + 1) * GRP):
                    fn(actv[:, i, c:c + 1], gel[:, i, c:c + 1], ACT.Copy, scale=gates[:, i, c:c + 1])\
                        .then_inc(actv_ready, 1)
                for c in range(g * GRP, (g + 1) * GRP):
                    act.wait_ge(actv_ready, u * TOPK + c + 1)
                    act.wait_ge(slot_free, u * TOPK + c + 1 + RING - DIAGS)
                    fn(diag[:, c % DIAGS, :], ident[:, :], ACT.Copy, scale=actv[:, i, c:c + 1])\
                        .then_inc(diag_ready, 1)

            def keep_x2T(t):
                for j in range(2):
                    act.wait_ge(x2_tr, 2 * t + j + 1)
                    fn(x1T[:, 4 * j:4 * j + 4, t * P:(t + 1) * P],
                       ps[:, x2_bank(t) + j, :].rearrange("p (k n) -> p k n", k=4), ACT.Copy).then_inc(x2T_ready, 1)

            def gate_sigmoid(t, j):
                act.wait_ge(gate_in, 2 * t + j + 1)
                half = x1[:, t, j * HALF:(j + 1) * HALF]
                fn(half, half, ACT.Sigmoid).then_inc(gate_ready, 1)

            scaled_attn(0)
            sqrt_var(1)
            scaled_attn(1)
            keep_x1T(0)
            keep_query(0)
            gate_exp(0, 0)
            sqrt_var(1)
            keep_x1T(1)
            keep_query(1)

            def unit(h, t, last_head, first_head=False):
                u = h * NT + t
                for g in range(NG):
                    activate(u, t, g)
                    if first_head and t == NT - 1 and 2 <= g < 2 + len(gains):
                        keep_gain(g - 2)
                    leaving = first_head and t < 2
                    if leaving and g == 1:
                        scaled_attn(t + 2)
                    if leaving and g == 4:
                        sqrt_var(1)
                    if leaving and g == 6:
                        keep_x1T(t + 2)
                    if g == 4 and not (last_head and t == NT - 1):
                        gate_exp(u + 1, (t + 1) % NT)
                    if g == (7 if leaving else 1 if last_head else 5) and not (last_head and t + 2 >= NT):
                        keep_query(u + 2)
                    if last_head and t:
                        if g == 1 or (g in (3, 5) and t == NT - 1):
                            sqrt_var(1)
                        if g == 3:
                            keep_x2T(t - 1)
                        if g == 7:
                            gate_sigmoid(t - 1, 0)
                            gate_sigmoid(t - 1, 1)

            for t in range(NT):
                unit(0, t, False, True)
            with act.Fori(1, PH - 1) as h:
                for t in range(NT):
                    unit(h, t, False)
            for t in range(NT):
                unit(PH - 1, t, True)
            sqrt_var(1)
            keep_x2T(NT - 1)
            sqrt_var(1)
            gate_sigmoid(NT - 1, 0)
            gate_sigmoid(NT - 1, 1)
            sqrt_var(1)

        @block.vector
        def _(dve):
            v = nc.vector
            seen = Counter(dve_at)

            def step(ins):
                seen.inc(ins)
                dve.wait_ge(dve_at, seen.base + seen.n)

            def step_to_max(ins):
                seen.inc(ins)
                hold(dve, dve_at, seen.base + seen.n, dve_passed)

            asked = Counter(var_ready)

            def rsqrt(n, out_):
                dve.wait_ge(std_ready, asked.n)
                step(v.reciprocal(rinv[:, 0:n], std[:, 0:n]))
                step(v.tensor_tensor(rtmp[:, 0:n], rinv[:, 0:n], rinv[:, 0:n], ALU.mult))
                step(v.scalar_tensor_tensor(out=rtmp[:, 0:n], in0=rtmp[:, 0:n], scalar=-0.5, in1=var_e[:, 0:n],
                                            op0=ALU.mult, op1=ALU.mult))
                step(v.scalar_tensor_tensor(out=out_, in0=rtmp[:, 0:n], scalar=1.5, in1=rinv[:, 0:n],
                                            op0=ALU.add, op1=ALU.mult))

            def layer_norm_stats(src, k=0):
                for j in range(2):
                    step(v.bn_stats(stats[:, j, :], src[:, j * HALF:(j + 1) * HALF]))
                step(v.bn_aggr(aggr[:, k, :], stats[:, 0:2, :]))
                asked.inc(v.tensor_scalar_add(var_e[:, 0:1], aggr[:, k, 1:2], EPS))

            def centre(src, g, k=0):
                step(v.scalar_tensor_tensor(out=src, in0=src, scalar=aggr[:, k, 0:1], in1=g,
                                            op0=ALU.subtract, op1=ALU.mult))

            def rescale(src, b, done):
                rsqrt(1, rstd[:, 0:1])
                for j in range(2):
                    cols = slice(j * HALF, (j + 1) * HALF)
                    v.scalar_tensor_tensor(out=src[:, cols], in0=src[:, cols], scalar=rstd[:, 0:1], in1=b[:, cols],
                                           op0=ALU.mult, op1=ALU.add).then_inc(done, 1)

            for b in range(WB):
                dve.wait_ge(proj_done, 4 + b + 1)
                v.tensor_copy(kT[:, b, :], ps[:, 4 + b, :]).then_inc(dve_evac, 1)
            for t in range(NT):
                dve.wait_ge(proj_done, 8 + t + 1)
                v.tensor_copy(v_tok[:, t, :], ps[:, t, :]).then_inc(dve_evac, 1)
            for t in range(NT):
                dve.wait_ge(act_evac, 4 + t + 1)
                step(v.bn_stats(stats[:, t, :], gv[:, t, :]))
                step(v.bn_aggr(aggr[:, t, :], stats[:, t, :]))
            asked.inc(v.tensor_scalar_add(var_e[:, 0:NT], aggr[:, 0:NT, 1], EPS))
            dve.wait_ge(small_in, 16 * 7)

            def gv_norm(t):
                step(v.scalar_tensor_tensor(out=gv[:, t, :], in0=gv[:, t, :], scalar=aggr[:, t, 0:1], in1=vn_g,
                                            op0=ALU.subtract, op1=ALU.mult))
                i = v.scalar_tensor_tensor(out=gv[:, t, :], in0=gv[:, t, :], scalar=rstd[:, t:t + 1], in1=vn_b,
                                           op0=ALU.mult, op1=ALU.add)
                if t == NT - 1:
                    i.then_inc(gvn_ready, 1)

            def add_squares(kind, b):
                first = squares[:, kind * WB, :]
                if b > 1:
                    dve.wait_ge(sq_added, kind * (WB - 1) + b - 1)
                v.tensor_tensor(first, first, squares[:, kind * WB + b, :], ALU.add).then_inc(sq_added, 1)

            def take_pair(b):
                dve.wait_ge(attn_sq, b + 1)
                v.tensor_scalar(attnT[:, b, :], ps[:, 6 + b % 2, :], gA[:, b:b + 1], None, ALU.mult)\
                    .then_inc(attn_scaled, 1)
                if b:
                    add_squares(0, b)

            for h in range(AH):
                z = psf[:, (h % 2) * 1536:(h % 2) * 1536 + ZCOLS]
                dve.wait_ge(log_ready, h + 1)
                v.scalar_tensor_tensor(out=l_buf[:, h % 2, :], in0=z, scalar=0.0, in1=e_buf[:, h % 3, :],
                                       op0=ALU.max, op1=ALU.add).then_inc(l_ready, 1)
                if h == 0:
                    rsqrt(NT, rstd[:, 0:NT])
                if h % 2 == 0:
                    gv_norm(h // 2)
                if h % 2 == 1 and h >= 3:
                    take_pair(h // 2 - 1)
            take_pair(WB - 1)
            for b in range(WB):
                dve.wait_ge(mixed_done, b + 1)
                m = ps[:, b, :].rearrange("p (t n) -> p t n", t=NT)
                bias = bs_b[:, b, :].unsqueeze(1).to_broadcast([P, NT, P])
                dst = l_buf[:, b % 2, 0:S]
                step(v.tensor_tensor(dst.rearrange("p (t n) -> p t n", t=NT), m, bias, ALU.add))
                v.tensor_tensor(guT[:, b, :], dst, guT[:, b, :], ALU.mult).then_inc(gm_ready, 1)
                if b >= 2:
                    dve.wait_ge(gm_sq, b)
                    add_squares(1, b - 1)
            dve.wait_ge(gm_sq, WB)
            add_squares(1, WB - 1)
            dve.wait_ge(ssq_done, 1)
            asked.inc(v.tensor_scalar(var_e[:, 0:2 * NT], ps[:, 4, 0:2 * NT], 1.0 / AW, EPS, ALU.mult, ALU.add))
            rsqrt(2 * NT, rsn[:, :])
            v.tensor_copy(rtmp[:, 0:1], rsn[:, 0:1]).then_inc(rms_ready, 1)
            v.tensor_copy(rtmp[:, 1:2], rsn[:, 0:1]).then_inc(sum_free, 2)
            dve.wait_ge(x_in, 16)
            dve.wait_ge(ln1_in, 32)
            def add_attn(t):
                xt = x1[:, t, :]
                dve.wait_ge(pa_scaled, t + 1)
                step(v.scalar_tensor_tensor(out=xt, in0=x_nat[:, t, :], scalar=ALPHA, in1=xt,
                                            op0=ALU.mult, op1=ALU.add))

            def add_gmlp(t):
                xt = x1[:, t, :]
                dve.wait_ge(pg_done, t + 1)
                step(v.scalar_tensor_tensor(out=xt, in0=psf[:, pg_bank(t) * 512:pg_bank(t) * 512 + D],
                                            scalar=rsn[:, NT + t:NT + t + 1], in1=xt,
                                            op0=ALU.mult, op1=ALU.add))
                layer_norm_stats(xt)
                centre(xt, ln1_g)

            def make_x1(t):
                add_attn(t)
                add_gmlp(t)
                rescale(x1[:, t, :], ln1_b, x1_ready)

            def rank_keys(u, half):
                if half == 0:
                    hold(dve, score_done, u + 1, dve_passed)
                s = ps[:, 7, half * NKEY:(half + 1) * NKEY]
                step_to_max(v.max(out=top[:, half, 0:8], in_=s))
                v.max_index(out=topi[:, half, 0:8], in_max=top[:, half, 0:8], in_values=s)
                step_to_max(v.match_replace(out=left[:, half, :], in_to_replace=top[:, half, 0:8], in_values=s,
                                            imm_value=NEG))
                step_to_max(v.max(out=top[:, half, 8:16], in_=left[:, half, :]))
                k = v.max_index(out=topi[:, half, 8:16], in_max=top[:, half, 8:16], in_values=left[:, half, :])
                if half == 0:
                    step_to_max(k)
                else:
                    k.then_inc(score_used, 1)

            def rank_sums(u, t):
                i = t % NT
                first = top[:, 0, :].unsqueeze(2).to_broadcast([P, TOPK, TOPK])
                second = top[:, 1, :].unsqueeze(1).to_broadcast([P, TOPK, TOPK])
                step(v.tensor_tensor(cand[:, :].rearrange("p (x y) -> p x y", x=TOPK), first, second, ALU.add))
                dve.wait_ge(score_used, u + 1)
                step_to_max(v.tensor_copy(topf[:, :, :], topi[:, :, :]))
                step_to_max(v.max(out=best[:, i, 0:8], in_=cand[:, :]))
                v.max_index(out=besti[:, 0:8], in_max=best[:, i, 0:8], in_values=cand[:, :])
                step_to_max(v.match_replace(out=cleft[:, :], in_to_replace=best[:, i, 0:8], in_values=cand[:, :],
                                     imm_value=NEG))
                step_to_max(v.max(out=best[:, i, 8:16], in_=cleft[:, :]))
                step(v.max_index(out=besti[:, 8:16], in_max=best[:, i, 8:16], in_values=cleft[:, :]))

            def rank_ids(u, t):
                i = t % NT
                v.tensor_scalar(negmax[:, i:i + 1], best[:, i, 0:1], -1.0, None, ALU.mult)
                v.tensor_scalar(nib[:, 0, :], besti[:, :], 4, None, ALU.logical_shift_right)
                step(v.tensor_scalar(nib[:, 1, :], besti[:, :], 15, None, ALU.bitwise_and))
                step(v.tensor_copy(nibf[:, :, :], nib[:, :, :]))
                want = nibf[:, :, :].unsqueeze(3).to_broadcast([P, 2, TOPK, TOPK])
                lanes = iota16[:, :].unsqueeze(1).unsqueeze(1).to_broadcast([P, 2, TOPK, TOPK])
                vals = topf[:, :, :].unsqueeze(2).to_broadcast([P, 2, TOPK, TOPK])
                step(v.tensor_tensor(hot[:, :, :, :], lanes, want, ALU.is_equal))
                step(v.tensor_tensor(hot[:, :, :, :], hot[:, :, :, :], vals, ALU.mult))
                step(v.reduce_sum(pick[:, :, :], hot[:, :, :, :], AX.X))
                v.scalar_tensor_tensor(out=ids[:, i, :], in0=pick[:, 0, :], scalar=float(NKEY), in1=pick[:, 1, :],
                                       op0=ALU.mult, op1=ALU.add).then_inc(ids_ready, 1)

            def norm_gates(u, t):
                i = t % NT
                dve.wait_ge(exp_ready, u + 1)
                step(v.reciprocal(erec[:, i:i + 1], esum[:, i:i + 1]))
                v.tensor_scalar(gates[:, i, :], expv[:, i, :], erec[:, i:i + 1], None, ALU.mult)\
                    .then_inc(gates_ready, 1)

            def dots(u, t, g):
                for c in range(g * GRP, (g + 1) * GRP):
                    r = rows[:, c % RING, 0:D]
                    dve.wait_ge(rows_in[c % RING], u * (16 * TOPK // RING) + 16 * (c // RING + 1))
                    v.tensor_tensor_reduce(out=r, in0=r, in1=x1[:, t, :], scale=1.0, scalar=0.0,
                                           op0=ALU.mult, op1=ALU.add,
                                           accum_out=hid[:, t, c:c + 1]).then_inc(dots_done, 1)

            def add_unit(u, t, first_head=False):
                dve.wait_ge(slot_free, u * TOPK + TOPK + RING)
                b = 2 * (t % 2) * 512
                if first_head:
                    v.tensor_copy(acc[:, t, :], psf[:, b:b + D]).then_inc(sum_free, 1)
                else:
                    v.tensor_tensor(acc[:, t, :], psf[:, b:b + D], acc[:, t, :], ALU.add).then_inc(sum_free, 1)

            def residual(t):
                dve.wait_ge(sum_free, NT * (PH - 1) + t - NT + 3)
                step(v.scalar_tensor_tensor(out=acc[:, t, :], in0=x1[:, t, :], scalar=ALPHA, in1=acc[:, t, :],
                                            op0=ALU.mult, op1=ALU.add))

            def second_norm(t):
                dve.wait_ge(sum_free, 2 + NT * PH - NT + t + 1)
                layer_norm_stats(acc[:, t, :], NT)
                centre(acc[:, t, :], ln2_g, NT)

            def open_gate(t, j):
                half = x1[:, t, j * HALF:(j + 1) * HALF]
                dve.wait_ge(gate_done, 2 * t + j + 1)
                v.tensor_tensor(half, ps[:, gate_bank(t) + j, :], b_gate[:, j * HALF:(j + 1) * HALF], ALU.add)\
                    .then_inc(gate_in, 1)

            def add_embedding(t, j):
                half = x1[:, t, j * HALF:(j + 1) * HALF]
                cols = slice(j * HALF, (j + 1) * HALF)
                dve.wait_ge(gate_ready, 2 * t + j + 1)
                dve.wait_ge(embedding_done, 2 * t + j + 1)
                v.tensor_tensor(half, ps[:, embedding_bank(t) + j, :], half, ALU.mult).then_inc(ple_used, 1)
                dve.wait_ge(ple_used, 2 * t + j + 1)
                step(v.scalar_tensor_tensor(out=acc[:, t, cols], in0=acc[:, t, cols], scalar=ALPHA, in1=half,
                                            op0=ALU.mult, op1=ALU.add))
                step(v.bn_stats(stats[:, 2 + j, :], acc[:, t, cols]))

            def add_embeddings(t):
                for j in range(2):
                    add_embedding(t, j)
                step(v.bn_aggr(aggr[:, t, :], stats[:, 2:4, :]))

            def third_norm(t):
                asked.inc(v.tensor_scalar_add(var_e[:, 0:1], aggr[:, t, 1:2], EPS))
                centre(acc[:, t, :], ln3_g, t)

            make_x1(0)
            for half in range(2):
                rank_keys(0, half)
            rank_sums(0, 0)
            rank_ids(0, 0)
            make_x1(1)
            norm_gates(0, 0)

            def unit(h, t, last_head, first_head=False):
                u = h * NT + t
                more = not (last_head and t == NT - 1)
                for g in range(NG):
                    dots(u, t, g)
                    if g == 1 and last_head and t >= 2:
                        add_embeddings(t - 2)
                    if g == 1 and t:
                        add_unit(u - 1, t - 1, first_head)
                        if last_head:
                            if t == 1:
                                dve.wait_ge(gain_kept, len(gains))
                            second_norm(t - 1)
                    if last_head and t and g == 2:
                        rescale(acc[:, t - 1, :], ln2_b, x2_ready)
                    if more and last_head and g in (1, 2):
                        rank_keys(u + 1, g - 1)
                    if more and not last_head and g in (0, 1):
                        rank_keys(u + 1, g)
                    if more and g == (3 if last_head else 2):
                        rank_sums(u + 1, t + 1)
                    if more and g == (4 if last_head else 3):
                        rank_ids(u + 1, t + 1)
                    if more and g == 5:
                        norm_gates(u + 1, t + 1)
                    if first_head and t < 2:
                        if g == 3:
                            add_attn(t + 2)
                        if g == 4:
                            add_gmlp(t + 2)
                        if g == 5:
                            rescale(x1[:, t + 2, :], ln1_b, x1_ready)
                    if last_head and t == NT - 1:
                        if g in (3, 5):
                            third_norm(g // 2 - 1)
                        if g in (4, 6):
                            rescale(acc[:, g // 2 - 2, :], ln3_b, out_ready)
                    if last_head and t and g in (5, 6):
                        open_gate(t - 1, g - 5)
                    if last_head and g == 7:
                        residual(t)
                if t == NT - 1:
                    add_unit(u, t, first_head)

            for t in range(NT):
                unit(0, t, False, True)
            before = seen.n
            with dve.Fori(1, PH - 1) as h:
                seen.base, seen.n = (h - 1) * HEAD_STEPS + before, 0
                for t in range(NT):
                    unit(h, t, False)
                assert seen.n == HEAD_STEPS
            seen.base, seen.n = 0, before + HEAD_STEPS * (PH - 2)
            for t in range(NT):
                unit(PH - 1, t, True)
            second_norm(NT - 1)
            rescale(acc[:, NT - 1, :], ln2_b, x2_ready)
            add_embeddings(NT - 2)
            third_norm(NT - 2)
            rescale(acc[:, NT - 2, :], ln3_b, out_ready)
            for j in range(2):
                open_gate(NT - 1, j)
                add_embedding(NT - 1, j)
            step(v.bn_aggr(aggr[:, NT - 1, :], stats[:, 2:4, :]))
            third_norm(NT - 1)
            rescale(acc[:, NT - 1, :], ln3_b, out_ready)


def kernel(**inputs):
    import concourse.bacc as _bacc
    from concourse.bass_utils import run_bass_kernel_spmd as _run

    f = {k: np.asarray(x) for k, x in inputs.items()}

    def chunks(w):
        return w.reshape(-1, P, w.shape[-1]).transpose(1, 0, 2)

    def blocks(w):
        return w.reshape(KD, P, WB, P).transpose(1, 2, 0, 3).reshape(P, -1)

    w = f["w_in"][0]
    x = f["x"][0]
    arrays = {
        "xT": chunks(x.T),
        "x": x.reshape(NT, P, D).transpose(1, 0, 2),
        "w_q": blocks(w[:, 0:AW]),
        "w_k": blocks(w[:, AW:2 * AW]),
        "w_v": chunks(w[:, 2 * AW:3 * AW]).reshape(P, -1),
        "w_gu": blocks(w[:, 3 * AW:4 * AW]),
        "w_gv": chunks(w[:, 4 * AW:5 * AW]).reshape(P, -1),
        "wsT": f["gmlp_ws"][0].transpose(2, 0, 1),
        "gA": f["attn_out_g"][0].reshape(WB, P).T,
        "gG": f["gmlp_out_g"][0].reshape(WB, P).T,
        "w_out": chunks(f["w_out"][0]),
        "wq": f["peer_wq"][0].reshape(KD, P, PH, QD).transpose(2, 1, 0, 3),
        "subk": f["peer_subkeys"][0].transpose(3, 0, 1, 2).reshape(P, -1),
        "uv": np.concatenate([f["peer_u"][0], f["peer_v"][0]], axis=1),
        "w_gate": chunks(f["ple_wgate"][0]),
        "w_proj": chunks(f["ple_wproj"][0]),
        "pT": chunks(f["p"][0, 0].T),
    }
    for name in ("gmlp_vn_g", "gmlp_vn_b", "gmlp_bs", "ln1_g", "ln1_b", "ln2_g", "ln2_b", "ln3_g", "ln3_b",
                 "ple_bgate"):
        arrays[name] = f[name]
    nc = _bacc.Bacc("TRN2", target_bir_lowering=False, num_devices=1)
    data, aps = {}, {}
    for name, array in arrays.items():
        data[f"in_{name}"] = np.ascontiguousarray(array)
        aps[name] = nc.dram_tensor(f"in_{name}", array.shape, FP32, kind="ExternalInput").ap()
    out = nc.dram_tensor("out_0", (1, S, D), FP32, kind="ExternalOutput").ap()
    build(nc, aps, out)
    return _run(nc, [data], core_ids=[0]).results[0]["out_0"]
```
